# Optimizing a Trainium2 kernel written in Bass

```python
import math
import jax, jax.numpy as jnp
from jax import lax
import numpy as np

D_MODEL = 1024
BATCH = 1
SEQ = 512
DEPTH = 2

PLE_DIM = 256
N_A = DEPTH // 2
N_B = DEPTH - N_A
SB_HEAD_DIM = 64
SB_HEADS = D_MODEL // SB_HEAD_DIM
SB_WIDTH = SB_HEADS * SB_HEAD_DIM
DIFF_QK_DIM = 64
DIFF_V_DIM = 2 * DIFF_QK_DIM
DIFF_HEADS = D_MODEL // DIFF_V_DIM
DIFF_QK_WIDTH = DIFF_HEADS * DIFF_QK_DIM
DIFF_WIDTH = DIFF_HEADS * DIFF_V_DIM
N_BUCKETS = 32
MAX_DISTANCE = 128
BLOCK_Q = 128
EPS = 1e-6
NEG_INF = -1e30

kernel_name = "yoco_stickbreak_diffattn_hybrid"

def rmsnorm(x, g):
    xf = x.astype(jnp.float32)
    y = xf * lax.rsqrt(jnp.mean(xf * xf, axis=-1, keepdims=True) + EPS)
    return (y * g.astype(jnp.float32)).astype(x.dtype)

def t5_bucket(dist):
    n = jnp.maximum(dist, 0)
    max_exact = N_BUCKETS // 2
    nf = jnp.maximum(n, 1).astype(jnp.float32)
    large = max_exact + (jnp.log(nf / max_exact) / math.log(MAX_DISTANCE / max_exact)
                         * (N_BUCKETS - max_exact)).astype(jnp.int32)
    large = jnp.minimum(large, N_BUCKETS - 1)
    return jnp.where(n < max_exact, n, large)

def to_blocks(a):
    b, s, h, d = a.shape
    return a.reshape(b, s // BLOCK_Q, BLOCK_Q, h, d).transpose(1, 0, 2, 3, 4)

def from_blocks(a):
    nb, b, tq, h, d = a.shape
    return a.transpose(1, 0, 2, 3, 4).reshape(b, nb * tq, h, d)

def stick_breaking_attention(q, k, v):
    s_len = k.shape[1]
    scale = 1.0 / math.sqrt(q.shape[-1])
    key_pos = jnp.arange(s_len)

    def block(args):
        qb, t0 = args
        z = jnp.einsum('bqhd,bkhd->bhqk', qb, k) * scale
        q_pos = t0 + jnp.arange(BLOCK_Q)
        past = key_pos[None, :] < q_pos[:, None]
        log_1m = jnp.where(past, jax.nn.log_sigmoid(-z), 0.0)
        rev = lax.cumsum(log_1m, axis=3, reverse=True)
        after = jnp.concatenate([rev[..., 1:], jnp.zeros_like(rev[..., :1])], axis=-1)
        w = jnp.where(past, jnp.exp(jax.nn.log_sigmoid(z) + after), 0.0)
        return jnp.einsum('bhqk,bkhd->bqhd', w, v)

    nb = s_len // BLOCK_Q
    t0s = jnp.arange(nb, dtype=jnp.int32) * BLOCK_Q
    return from_blocks(lax.map(block, (to_blocks(q), t0s)))

def differential_attention(q1, q2, k1, k2, v, lam, rel_bias):
    s_len = k1.shape[1]
    scale = 1.0 / math.sqrt(q1.shape[-1])
    key_pos = jnp.arange(s_len)
    table = rel_bias.astype(jnp.float32)

    def block(args):
        q1b, q2b, t0 = args
        q_pos = t0 + jnp.arange(BLOCK_Q)
        dist = q_pos[:, None] - key_pos[None, :]
        causal = dist >= 0
        bias = jnp.transpose(table[t5_bucket(dist)], (2, 0, 1))
        s1 = jnp.einsum('bqhd,bkhd->bhqk', q1b, k1) * scale + bias
        s2 = jnp.einsum('bqhd,bkhd->bhqk', q2b, k2) * scale + bias
        a1 = jax.nn.softmax(jnp.where(causal, s1, NEG_INF), axis=-1)
        a2 = jax.nn.softmax(jnp.where(causal, s2, NEG_INF), axis=-1)
        return jnp.einsum('bhqk,bkhe->bqhe', a1 - lam * a2, v)

    nb = s_len // BLOCK_Q
    t0s = jnp.arange(nb, dtype=jnp.int32) * BLOCK_Q
    return from_blocks(lax.map(block, (to_blocks(q1), to_blocks(q2), t0s)))

def setup_inputs(seed: int = 0) -> dict:
    key = jax.random.key(seed)
    ks = jax.random.split(key, 18)

    def nrm(k, shape, scale):
        return jax.random.normal(k, shape, jnp.float32) * scale

    def gain(k, shape):
        return 1.0 + 0.02 * jax.random.normal(k, shape, jnp.float32)

    fan = D_MODEL ** -0.5
    return {
        "x": nrm(ks[0], (BATCH, SEQ, D_MODEL), 1.0),
        "p": nrm(ks[1], (DEPTH, BATCH, SEQ, PLE_DIM), 1.0),
        "attn_norm": gain(ks[2], (DEPTH, D_MODEL)),
        "w_in_a": nrm(ks[3], (N_A, D_MODEL, 4 * SB_WIDTH), fan),
        "w_out_a": nrm(ks[4], (N_A, SB_WIDTH, D_MODEL), SB_WIDTH ** -0.5),
        "kv_norm": gain(ks[5], (D_MODEL,)),
        "w_kv": nrm(ks[6], (D_MODEL, 2 * DIFF_QK_WIDTH + DIFF_WIDTH), fan),
        "w_q_b": nrm(ks[7], (N_B, D_MODEL, 2 * DIFF_QK_WIDTH + DIFF_WIDTH), fan),
        "diff_lambda": nrm(ks[8], (N_B, 4, DIFF_QK_DIM), 0.1),
        "diff_subln": gain(ks[9], (N_B, DIFF_V_DIM)),
        "w_out_b": nrm(ks[10], (N_B, DIFF_WIDTH, D_MODEL), DIFF_WIDTH ** -0.5),
        "rel_bias": nrm(ks[11], (N_BUCKETS, DIFF_HEADS), 0.5),
        "ple_norm": gain(ks[12], (DEPTH, D_MODEL)),
        "w_ple_proj": nrm(ks[13], (DEPTH, PLE_DIM, D_MODEL), PLE_DIM ** -0.5),
        "w_ple_gate": nrm(ks[14], (DEPTH, D_MODEL, D_MODEL), fan),
        "final_norm": gain(ks[15], (D_MODEL,)),
    }

def reference(x, p, attn_norm, w_in_a, w_out_a, kv_norm, w_kv, w_q_b, diff_lambda, diff_subln,
              w_out_b, rel_bias, ple_norm, w_ple_proj, w_ple_gate, final_norm):
    b, s, _ = x.shape
    h = x
    shared_k1 = shared_k2 = shared_v = None
    for i in range(DEPTH):
        if i < N_A:
            hn = rmsnorm(h, attn_norm[i])
            proj = hn @ w_in_a[i]
            q, k, v, g = jnp.split(proj, 4, axis=-1)
            q, k, v = (t.reshape(b, s, SB_HEADS, SB_HEAD_DIM).astype(jnp.float32) for t in (q, k, v))
            o = stick_breaking_attention(q, k, v).reshape(b, s, SB_WIDTH).astype(h.dtype)
            h = h + (o * jax.nn.silu(g)) @ w_out_a[i]
        else:
            j = i - N_A
            if i == N_A:
                kv = rmsnorm(h, kv_norm) @ w_kv
                k1, k2, vv = jnp.split(kv, [DIFF_QK_WIDTH, 2 * DIFF_QK_WIDTH], axis=-1)
                shared_k1 = k1.reshape(b, s, DIFF_HEADS, DIFF_QK_DIM).astype(jnp.float32)
                shared_k2 = k2.reshape(b, s, DIFF_HEADS, DIFF_QK_DIM).astype(jnp.float32)
                shared_v = vv.reshape(b, s, DIFF_HEADS, DIFF_V_DIM).astype(jnp.float32)
            hn = rmsnorm(h, attn_norm[i])
            qg = hn @ w_q_b[j]
            q1, q2, g = jnp.split(qg, [DIFF_QK_WIDTH, 2 * DIFF_QK_WIDTH], axis=-1)
            q1 = q1.reshape(b, s, DIFF_HEADS, DIFF_QK_DIM).astype(jnp.float32)
            q2 = q2.reshape(b, s, DIFF_HEADS, DIFF_QK_DIM).astype(jnp.float32)
            lam_init = 0.8 - 0.6 * math.exp(-0.3 * i)
            lp = diff_lambda[j].astype(jnp.float32)
            lam = jnp.exp(jnp.sum(lp[0] * lp[1])) - jnp.exp(jnp.sum(lp[2] * lp[3])) + lam_init
            o = differential_attention(q1, q2, shared_k1, shared_k2, shared_v, lam, rel_bias)
            o = rmsnorm(o, diff_subln[j]) * (1.0 - lam_init)
            o = o.reshape(b, s, DIFF_WIDTH).astype(h.dtype)
            h = h + (o * jax.nn.silu(g)) @ w_out_b[j]
        gate = jax.nn.sigmoid(rmsnorm(h, ple_norm[i]) @ w_ple_gate[i])
        h = h + gate * (p[i] @ w_ple_proj[i])
    return rmsnorm(h, final_norm)


_drawn_inputs = setup_inputs


def setup_inputs(seed=0):
    import zlib

    import numpy as np

    out = dict(_drawn_inputs(seed))
    spreads = {}
    factors = {'attn_norm': 3.943,
     'kv_norm': 6.016,
     'diff_subln': 25.184,
     'ple_norm': 41.932,
     'final_norm': 8.164}
    for name, (base, spread) in spreads.items():
        noise = np.random.default_rng([zlib.crc32(name.encode()), seed]).standard_normal(out[name].shape)
        drawn = base * np.exp(spread * noise) if base else spread * noise
        out[name] = __import__('jax').numpy.asarray(drawn.astype(out[name].dtype))
    for name, factor in factors.items():
        out[name] = (out[name] * factor).astype(out[name].dtype)
    return out
```

```python
from contextlib import ExitStack
import math

import numpy as np
import concourse.bass as bass
from concourse import mybir

F32 = mybir.dt.float32
F32R = mybir.dt.float32r
ALU = mybir.AluOpType
ACT = mybir.ActivationFunctionType
AX = mybir.AxisListType

D = 1024
S = 512
NT = D // 128
DP = 256
HEADS_A = 16
HEADS_B = 8
NB = 32
EPS = 1e-6
LAM_INIT = 0.8 - 0.6 * math.exp(-0.3 * 1)
NEG = -1e30
UNIT = 1024

U_G, U_V, U_Q, U_O, U_P, U_T, U_LAYER = 0, 8, 16, 32, 40, 44, 52
R_G, R_Q, R_O, R_P, R_T, R_LAYER = 0, 8, 24, 32, 40, 48
UNITS = 2 * U_LAYER

BW = 640
GROUPS = [[(3, 0), (2, 128)], [(1, 0)], [(0, 0)]]
GCOLS = [384, 384, 512]
NGA = 3 * HEADS_A
NSB = 4 * HEADS_B


def build(nc, xT, pT, w_units, gains, subln, lamp, table, onehot, scratch, outT):
    with ExitStack() as ctx:
        def sb(name, shape, dt=F32, where=ctx):
            return where.enter_context(nc.sbuf_tensor(name, shape, dt))

        def sem(name):
            return ctx.enter_context(nc.semaphore(name))

        bank = [ctx.enter_context(nc.psum_tensor(f"bank{i}", [128, 512], F32)) for i in range(8)]

        h = sb("h", [128, NT * S])
        ph = [sb(f"split{i}_hi", [128, NT * S], F32R) for i in range(2)]
        pl = [sb(f"split{i}_lo", [128, NT * S], F32R) for i in range(2)]
        gp = sb("gp", [128, NT * S])
        wf = sb("w_f32", [128, 2, UNIT])
        wh = sb("w_hi", [128, 4, UNIT], F32R)
        wl = sb("w_lo", [128, 4, UNIT], F32R)
        vph = sb("v_cols_hi", [128, 2, 4, 128], F32R)
        vpl = sb("v_cols_lo", [128, 2, 4, 128], F32R)
        rms = sb("rms", [128, S])
        rmc = sb("rms_col", [128, 4])
        ssq = sb("ssq", [128, S])
        sq = sb("sq", [128, S])
        tmp = sb("tmp", [128, 2, S])
        ones = sb("ones", [128, 128])
        trif = sb("trif", [128, 128])
        gn = sb("gains_sb", [128, 6 * NT])
        sub = sb("subln_sb", [128, 1])
        lp = tmp[:, 0, 0:256].rearrange("p (a d) -> p a d", a=4)
        lpp = tmp[:, 1, 0:128].rearrange("p (a d) -> p a d", a=2)
        lam = sb("lam", [128, 4])
        tb = sb("table_sb", [NB + 1, HEADS_B])
        small = sb("small", [128, 16])

        tA, tB = ExitStack(), ExitStack()
        with tA:
            neg1 = sb("neg1", [128, 128], F32R, tA)
            past = sb("past", [128, 2, 128], F32, tA)
            tri = sb("tri", [128, 128], F32R, tA)
            asp = sb("sp", [128, 2, S], F32, tA)
            aw = sb("w_att", [128, 2, S], F32, tA)
            alh = sb("l_hi", [128, 4, S], F32R, tA)
            all_ = sb("l_lo", [128, 4, S], F32R, tA)
            awh = sb("wa_hi", [128, 2, S], F32R, tA)
            awl = sb("wa_lo", [128, 2, S], F32R, tA)
            aqk = [sb(n, [128, 2, S], F32R, tA) for n in ("a_qh", "a_ql", "a_kh", "a_kl")]
        with tB:
            e1 = sb("e1", [128, 2, S], F32, tB)
            e2 = sb("e2", [128, S], F32, tB)
            bt = sb("bias_tile", [128, 2, S], F32, tB)
            pth = sb("pt_hi", [128, 1280], F32R, tB)
            ptl = sb("pt_lo", [128, 1280], F32R, tB)
            bqk = [[sb(f"b_{n}{q}", [128, 2, S], F32R, tB) for q in "hl"] for n in ("k1", "k2", "q1", "q2")]
        pstage = [asp, e1]
        psplit = [(aqk[0], aqk[1]), (bqk[0][0], bqk[0][1])]
        oh = gp[0:NB + 1, 0:BW]
        toh = gp[0:NB + 1, 1024:1024 + BW]
        brow = [gp[:, 2048:2048 + BW], gp[:, 3072:3072 + BW]]

        s_x = [sem(f"s_x{i}") for i in range(4)]
        s_cst = sem("s_cst")
        s_lp = sem("s_lp")
        s_tb = sem("s_tb")
        s_wd = [sem(f"s_wd{i}") for i in range(2)]
        s_wg = sem("s_wg")
        s_wh = sem("s_wh")
        s_wl = sem("s_wl")
        s_one = sem("s_one")
        s_trf = sem("s_trf")
        s_past = sem("s_past")
        s_idn = sem("s_idn")
        s_unit = sem("s_unit")
        s_ple = sem("s_ple")
        s_read = sem("s_read")
        s_vres = sem("s_vres")
        s_vh = sem("s_vh")
        s_vl = sem("s_vl")
        s_xh = sem("s_xh")
        s_xl = sem("s_xl")
        s_sq = sem("s_sq")
        s_ss = sem("s_ss")
        s_stat = sem("s_stat")
        s_lnr = sem("s_lnr")
        s_rms = sem("s_rms")
        s_silu = sem("s_silu")
        s_silc = sem("s_silc")
        s_qh = sem("s_qh")
        s_qk = sem("s_qk")
        s_z = sem("s_z")
        s_abs = sem("s_abs")
        s_ex = sem("s_ex")
        s_ln = sem("s_ln")
        s_sp = sem("s_sp")
        s_ml = sem("s_ml")
        s_lh = sem("s_lh")
        s_ll = sem("s_ll")
        s_tri = sem("s_tri")
        s_we = sem("s_we")
        s_mw = sem("s_mw")
        s_ph = sem("s_ph")
        s_pl = sem("s_pl")
        s_av = sem("s_av")
        s_vp = sem("s_vp")
        s_og = sem("s_og")
        s_oh = sem("s_oh")
        s_ol = sem("s_ol")
        s_toh = sem("s_toh")
        s_brow = sem("s_brow")
        s_bst = sem("s_bst")
        s_bout = [sem(f"s_bout{i}") for i in range(2)]
        s_t0 = sem("s_t0")
        s_tb0 = sem("s_tb0")
        s_p = sem("s_p")
        s_pfh = sem("s_pfh")
        s_pfl = sem("s_pfl")
        s_sig = sem("s_sig")
        s_gm = sem("s_gm")
        s_hg = sem("s_hg")
        s_lam = sem("s_lam")
        s_lame = sem("s_lame")
        s_bt = [sem(f"s_bt{i}") for i in range(2)]
        s_s = sem("s_s")
        s_ttr = sem("s_ttr")
        s_nm = sem("s_nm")
        s_e = sem("s_e")
        s_rc = sem("s_rc")
        s_nr = sem("s_nr")
        s_e1n = sem("s_e1n")
        s_pr = sem("s_pr")
        s_tr = sem("s_tr")
        s_pth = sem("s_pth")
        s_pte = sem("s_pte")
        s_pv = sem("s_pv")
        s_osq = sem("s_osq")
        s_nst = sem("s_nst")
        s_nln = sem("s_nln")
        s_nrm = sem("s_nrm")
        s_on = sem("s_on")
        s_fin = sem("s_fin")
        s_out = sem("s_out")

        def X(which, k, part=slice(0, S)):
            return which[:, k * S + part.start:k * S + part.stop]

        def tile(buf, k):
            return buf[:, k * S:(k + 1) * S] if isinstance(k, int) else buf[:, bass.ds(k * S, S)]

        def gcol(g, k):
            return gn[:, g * NT + k:g * NT + k + 1] if isinstance(k, int) else gn[:, bass.ds(k + g * NT, 1)]

        def repeat(eng, unrolled, n, body):
            if unrolled:
                for it in range(n):
                    body(it)
            else:
                with eng.Fori(0, n) as it:
                    body(it)

        def gained(u):
            return u >= U_LAYER and u < U_LAYER + U_O

        block = ctx.enter_context(nc.Block())

        @block.sync
        def _(sp):
            sp.dma_start(gn[:, :], gains).then_inc(s_cst, 16)
            sp.dma_start(wf[:, 0, :], w_units[0]).then_inc(s_wd[0], 16)
            for i in range(4):
                sp.dma_start(h[:, 2 * i * S:(2 * i + 2) * S].rearrange("p (k t) -> p k t", k=2),
                             xT[2 * i:2 * i + 2].rearrange("k p t -> p k t")).then_inc(s_x[i], 16)
            sp.dma_start(wf[:, 1, :], w_units[1]).then_inc(s_wd[1], 16)
            with sp.Fori(1, UNITS // 2) as i:
                for slot in range(2):
                    sp.wait_ge(s_wl, i * 2 + (slot - 1))
                    sp.dma_start(wf[:, slot:slot + 1, :],
                                 w_units.rearrange("u p n -> p u n")[:, bass.ds(i * 2 + slot, 1), :]).then_inc(s_wd[slot], 16)
            for k in range(NT):
                sp.wait_ge(s_fin, k + 1)
                sp.dma_start(outT[k], tile(h, k)).then_inc(s_out, 16)
            sp.wait_ge(s_out, 16 * NT)
            for i in range(2):
                sp.wait_ge(s_bout[i], 16 * (HEADS_B // 2))

        @block.tensor
        def _(pe):
            def mm3(out, lh, ll, rh, rl, start, stop, last=None):
                pe.matmul(out, lhsT=lh, rhs=rh, start=start, stop=False, skip_group_check=True)
                pe.matmul(out, lhsT=lh, rhs=rl, start=False, stop=False, skip_group_check=True)
                return pe.matmul(out, lhsT=ll, rhs=rh, start=False, stop=stop, skip_group_check=True)

            def product(slot, which, k, start, stop):
                c = slice(128 * k, 128 * k + 128)
                return mm3(bank[slot % 2][:, :], wh[:, slot, c], wl[:, slot, c],
                           X(ph[which], k), X(pl[which], k), start, stop)

            def open_unit(u, slot, r):
                pe.wait_ge(s_wl, u + 1)
                if not isinstance(r, int) or r >= 2:
                    pe.wait_ge(s_read, r - 1)

            def unit(u, slot, which, r, ready=None):
                open_unit(u, slot, r)
                for k in range(NT):
                    if ready is not None:
                        pe.wait_ge(ready[0], ready[1] + k + 1)
                    last = product(slot, which, k, k == 0, k == NT - 1)
                last.then_inc(s_unit, 1)

            def stat(v):
                pe.wait_ge(s_ss, 9 * (v + 1))
                pe.matmul(bank[6][:, :], lhsT=ones[:, :], rhs=ssq[:, :], start=True, stop=True)
                for i in range(4):
                    last = pe.matmul(bank[7][:, i:i + 1], lhsT=ssq[:, 128 * i:128 * i + 128],
                                     rhs=ones[:, 0:1], start=(i == 0), stop=True, skip_group_check=True)
                last.then_inc(s_stat, 1)

            def values(L):
                with pe.Fori(0, 2) as half:
                    pe.wait_ge(s_vl, half * 4 + (8 * L + 1))
                    for j in range(4):
                        pe.wait_ge(s_wl, half * 4 + (L * U_LAYER + U_V + j + 1))
                        for i in range(4):
                            rows = slice(128 * i, 128 * i + 128)
                            for kk in range(2):
                                k = 2 * j + kk
                                c = slice(512 * kk, 512 * kk + 512)
                                last = mm3(bank[2 + i][:, :], X(ph[0], k, rows), X(pl[0], k, rows),
                                           wh[:, j, c], wl[:, j, c], k == 0, k == NT - 1)
                            if j == 3 and i < 3:
                                last.then_inc(s_vres, 1)
                        last.then_inc(s_unit, 1)

            def scores_a(a, am, P):
                g, hd = am % 3, (am // 3) % 2
                z = bank[2 + am % 4]
                par = (am // 6 + 0) % 2
                if am % 6 == 0:
                    pe.wait_ge(s_qk, P * 2)
                if not isinstance(a, int) or a >= 4:
                    pe.wait_ge(s_we, a - 3)
                qh, ql, kh, kl = aqk
                rows = slice(64 * hd, 64 * hd + 64)
                for n, (i, off) in enumerate(GROUPS[g]):
                    w = S - 128 * i
                    o = z[:, off:off + w]
                    kc, qc = slice(128 * i, 128 * i + 128), slice(128 * i, S)
                    last = mm3(o, kh[rows, par, kc], kl[rows, par, kc], qh[rows, par, qc], ql[rows, par, qc],
                               n == 0, True)
                last.then_inc(s_z, 1)

            def logsums(a, am):
                g = am % 3
                z = bank[2 + am % 4]
                pe.wait_ge(s_ll, a + 1)
                for i, off in GROUPS[g]:
                    for j in range(i, 4):
                        gj = 2 - j if j < 2 else 0
                        slot = (am - g + gj) % 4
                        src = dict(GROUPS[gj])[j]
                        w = S - 128 * j
                        o = z[:, off + 128 * (j - i):off + 128 * (j - i) + w]
                        st = tri if j == i else neg1
                        for part in (alh, all_):
                            last = pe.matmul(o, lhsT=st[:, :], rhs=part[:, slot, src:src + w], start=False,
                                             stop=True, skip_group_check=True)
                last.then_inc(s_tri, 1)

            def heads_a(a, am, P):
                g, hd = am % 3, (am // 3) % 2
                par = (am // 6) % 2
                o = bank[6 + hd]
                pe.wait_ge(s_pl, a + 1)
                if g == 0:
                    if hd == 0:
                        pe.wait_ge(s_vp, P * 2)
                    pe.wait_ge(s_og, P * 2 + (hd - 2))
                for i, off in GROUPS[g]:
                    w = S - 128 * i
                    last = mm3(o[:, 128 * i:S], vph[:, par, i, :], vpl[:, par, i, :],
                               awh[:, am % 2, off:off + w], awl[:, am % 2, off:off + w], i == 3, True)
                last.then_inc(s_av, 1)

            def block_a(P, Pm, dense, attend):
                a0 = P * 6 - 6 if isinstance(P, int) else P * 6 + (-6)
                u0 = P * 2 + U_Q
                for l in range(6):
                    am = (Pm * 6 + l - 6) % 12
                    a = a0 + l
                    if attend:
                        scores_a(a, am, P)
                    if dense and l < 4:
                        c = l // 2
                        slot = (2 * Pm + c) % 4
                        if l % 2 == 0:
                            open_unit(u0 + c, slot, P * 2 + (R_Q + c))
                        for k in range(4 * (l % 2), 4 * (l % 2) + 4):
                            last = product(slot, 0, k, k == 0, k == NT - 1)
                        if l % 2:
                            last.then_inc(s_unit, 1)
                    if attend and not (isinstance(a, int) and a < 2):
                        logsums(a - 2, (am - 2) % 12)
                    if attend and not (isinstance(a, int) and a < 3):
                        heads_a(a - 3, (am - 3) % 12, P if l >= 3 else P - 1)

            def tiles(L, U, R, which, ready, after=None):
                def body(it):
                    for j in range(4):
                        unit(it * 4 + (L * U_LAYER + U + j), j, which, it * 4 + (L * R_LAYER + R + j),
                             ready if j == 0 else None)
                        if after:
                            after(it * 4 + j)
                repeat(pe, after is not None, 2, body)

            def bias_row(hd):
                b = 2 + 2 * (hd % 2)
                pe.wait_ge(s_toh, hd + 1)
                if hd >= 2:
                    pe.wait_ge(s_bst, 2 * hd - 2)
                pe.matmul(bank[b][:, :], lhsT=ones[0:NB + 1, :], rhs=toh[:, 0:512], start=True, stop=True)
                pe.matmul(bank[b + 1][:, 0:BW - 512], lhsT=ones[0:NB + 1, :], rhs=toh[:, 512:BW],
                          start=True, stop=True).then_inc(s_brow, 1)

            def scores_b(a, P):
                hd, i = a // 4, a % 4
                if a % 8 == 0:
                    pe.wait_ge(s_qk, 2 * HEADS_A // 2 + 4 * P)
                rows = slice(64 * (hd % 2), 64 * (hd % 2) + 64)
                par = (P - 1) % 2
                w = 128 * i + 128
                qc = slice(128 * i, 128 * i + 128)
                for side in range(2):
                    kh, kl = bqk[side]
                    qh, ql = bqk[2 + side]
                    if a >= 1:
                        pe.wait_ge(s_ttr, 2 * a - 1 + side)
                    mm3(bank[2 + side][:, 0:w], qh[rows, par, qc], ql[rows, par, qc],
                        kh[rows, par, 0:w], kl[rows, par, 0:w], True, True).then_inc(s_s, 1)

            PT = [(4, 0, 0), (5, 0, 512), (6, 0, 1024), (5, 384, 896)]

            def transposes(a):
                hd, i = a // 4, a % 4
                pe.wait_ge(s_pr, a + 1)
                if i == 0 and hd > 0:
                    pe.wait_ge(s_pte, 3 * hd)
                for j in range(i + 1):
                    if j == 2 and i == 2 and hd > 0:
                        pe.wait_ge(s_nln, hd)
                    b, c, _ = PT[j]
                    c += 128 * (i - j)
                    last = pe.transpose(bank[b][:, c:c + 128], e1[:, a % 2, 128 * j:128 * j + 128], trif[:, :])
                last.then_inc(s_tr, 1)

            def head_b(hd):
                pe.wait_ge(s_pte, 3 * hd + 3)
                pe.wait_ge(s_vp, 2 * (HEADS_A // 2) + 2 * (hd + 1))
                if hd > 0:
                    pe.wait_ge(s_on, hd)
                for j in range(4):
                    w = S - 128 * j
                    _, _, c = PT[j]
                    last = mm3(bank[7][:, 128 * j:S], vph[:, hd % 2, j, :], vpl[:, hd % 2, j, :],
                               pth[:, c:c + w], ptl[:, c:c + w], j == 0, True)
                last.then_inc(s_pv, 1)

            def head_stat(hd):
                pe.wait_ge(s_osq, hd + 1)
                pe.matmul(bank[6][:, :], lhsT=ones[:, :], rhs=sq[:, :], start=True, stop=True).then_inc(s_nst, 1)

            def block_b(P):
                for l in range(8):
                    a = 8 * P + l - 8
                    if 0 <= a < NSB:
                        scores_b(a, P)
                    if P < 4 and l < 6:
                        for m in range(16 * l // 3, 16 * (l + 1) // 3):
                            c, k = m // 8, m % 8
                            if k == 0:
                                open_unit(U_LAYER + U_Q + 4 * P + c, c, R_LAYER + R_Q + 4 * P + c)
                            last = product(c, 0, k, k == 0, k == NT - 1)
                            if k == NT - 1:
                                last.then_inc(s_unit, 1)
                    tail_b(a)

            def tail_b(a):
                if 2 <= a < NSB + 2:
                    transposes(a - 2)
                if a >= 6 and (a - 6) % 4 == 0 and (a - 6) // 4 < HEADS_B:
                    head_b((a - 6) // 4)
                if a >= 7 and (a - 7) % 4 == 0:
                    head_stat((a - 7) // 4)

            def gate_project(L):
                v = 2 * L
                for n in range(NT):
                    unit(L * U_LAYER + U_G + n, n % 4, 0, L * R_LAYER + R_G + n,
                         (s_xl, 8 * v) if n == 0 else None)
                    if n == 0:
                        stat(v)

            def rest(L):
                base = L * U_LAYER
                tiles(L, U_O, R_O, 0, (s_ol, NT * L), bias_row if L == 0 else None)
                pe.wait_ge(s_pfl, L + 1)
                fh, fl = psplit[L]
                for n in range(4):
                    pe.wait_ge(s_wl, base + U_P + n + 1)
                    for nn in range(2):
                        pe.wait_ge(s_read, L * R_LAYER + R_P + 2 * n + nn - 1)
                        for kk in range(2):
                            c = slice(128 * (2 * nn + kk), 128 * (2 * nn + kk) + 128)
                            last = mm3(bank[nn][:, :], wh[:, n, c], wl[:, n, c], fh[:, kk, :], fl[:, kk, :],
                                       kk == 0, kk == 1)
                        last.then_inc(s_ple if nn == 0 else s_unit, 1)
                stat(2 * L + 1)
                tiles(L, U_T, R_T, 1, (s_xl, 8 * (2 * L + 1)))

            pe.wait_ge(s_one, 2)
            gate_project(0)
            values(0)
            block_a(0, 0, True, False)
            block_a(1, 1, True, True)
            with pe.Fori(1, 4) as it:
                block_a(it * 2, 0, True, True)
                block_a(it * 2 + 1, 1, True, True)
            block_a(8, 0, False, True)
            for a in range(NGA, NGA + 3):
                if a < NGA + 2:
                    logsums(a - 2, (a - 2) % 12)
                heads_a(a - 3, (a - 3) % 12, 8)
            rest(0)
            gate_project(1)
            values(1)
            pe.wait_ge(s_idn, 2)
            for P in range(5):
                block_b(P)
            for a in range(NSB, NSB + 4):
                tail_b(a)
            rest(1)
            stat(4)

        @block.scalar
        def _(act):
            def split_hi(u, slot, gain):
                if gain:
                    act.wait_ge(s_wg, u + (1 - U_LAYER))
                elif isinstance(u, int):
                    act.wait_ge(s_wd[slot % 2], 16 * (u // 2) + 16)
                act.wait_ge(s_unit, u - 3) if not isinstance(u, int) or u > 3 else None
                act.activation(wh[:, slot, :], wf[:, slot % 2, :], ACT.Copy).then_inc(s_wh, 1)

            def split_hi_loop(it, c, step, slot):
                act.wait_ge(s_wd[slot % 2], it * (8 * step) + (16 * (c // 2) + 16))
                act.wait_ge(s_unit, it * step + (c - 3))
                act.activation(wh[:, slot, :], wf[:, slot % 2, :], ACT.Copy).then_inc(s_wh, 1)

            def square(v, k, src):
                act.wait_ge(s_ss, k + (9 * v + 1))
                act.activation(sq[:, :], src, ACT.Square).then_inc(s_sq, 1)

            def norm(v):
                act.preload_act_table_set("natural_log_exp_and_others")
                act.wait_ge(s_stat, v + 1)
                act.activation(rms[:, :], bank[6][:, :], ACT.Ln, scale=1.0 / D, bias=EPS).then_inc(s_lnr, 1)
                act.activation(rmc[:, :], bank[7][:, 0:4], ACT.Ln, scale=1.0 / D, bias=EPS).then_inc(s_lnr, 1)
                act.wait_ge(s_lnr, 2 * v + 2)
                act.activation(rms[:, :], rms[:, :], ACT.Exp, scale=-0.5).then_inc(s_rms, 1)
                act.activation(rmc[:, :], rmc[:, :], ACT.Exp, scale=-0.5).then_inc(s_rms, 1)

            def gate_project(L):
                for n in range(NT):
                    u = L * U_LAYER + U_G + n
                    split_hi(u + 2, (u + 2) % 4, gained(u + 2))
                    if n == 0:
                        norm(2 * L)
                        if L == 0:
                            act.wait_ge(s_lam, 3)
                            act.activation(lam[:, 0:2], lam[:, 0:2], ACT.Exp).then_inc(s_lame, 1)
                        act.preload_act_table(ACT.Silu)
                    act.wait_ge(s_read, L * R_LAYER + R_G + n + 1)
                    if L == 1 and n == 0:
                        act.wait_ge(s_hg, NT)
                    act.activation(tile(gp, n), tmp[:, n % 2, :], ACT.Silu).then_inc(s_silu, 1)

            def values(L):
                act.wait_ge(s_rms, 4 * L + 2)
                for half in range(2):
                    for j in range(4):
                        c = L * U_LAYER + U_V + j + 2
                        slot = (j + 2) % 4
                        if L == 1:
                            act.wait_ge(s_wg, half * 4 + (c + 1 - U_LAYER))
                            act.wait_ge(s_unit, half * 4 + (c - 3))
                            act.activation(wh[:, slot, :], wf[:, slot % 2, :], ACT.Copy).then_inc(s_wh, 1)
                        else:
                            split_hi_loop(half, c, 4, slot)
                    for i in range(4):
                        if i < 3:
                            act.wait_ge(s_vres, half * 3 + (6 * L + i + 1))
                        else:
                            act.wait_ge(s_unit, half * 4 + (L * U_LAYER + U_V + 4))
                        act.activation(ph[1][:, 1024 * i + 512 * half:1024 * i + 512 * half + 512], bank[2 + i][:, :], ACT.Copy,
                                       scale=rmc[:, i:i + 1]).then_inc(s_vh, 1)

            def stream_hi(v, k, scale):
                act.activation(tile(ph[v % 2], k), tile(h, k), ACT.Copy, scale=scale).then_inc(s_xh, 1)

            def slot_a(a, am, P, Pm, l, dense, attend):
                qh, ql, kh, kl = aqk
                last = isinstance(a, int) and a >= NGA
                if attend and not (isinstance(a, int) and (a < 1 or a > NGA)):
                    b = (am - 1) % 12
                    act.wait_ge(s_ml, a)
                    if not (isinstance(a, int) and a < 3):
                        act.wait_ge(s_tri, a - 2)
                    act.activation(alh[:, b % 4, 0:GCOLS[b % 3]], asp[:, b % 2, 0:GCOLS[b % 3]],
                                   ACT.Copy).then_inc(s_lh, 1)
                if attend and not last:
                    w = GCOLS[am % 3]
                    buf = asp[:, am % 2, 0:w]
                    act.wait_ge(s_z, a + 1)
                    if not (isinstance(a, int) and a < 2):
                        act.wait_ge(s_ll, a - 1)
                    act.activation(buf, bank[2 + am % 4][:, 0:w], ACT.Abs).then_inc(s_abs, 1)
                if dense and l in (0, 2):
                    c = U_Q + 2 + l // 2
                    slot = (2 * Pm + 2 + l // 2) % 4
                    if isinstance(P, int):
                        split_hi(2 * P + c, slot, False)
                    else:
                        it, b = P_it[0]
                        split_hi_loop(it, c + 2 * b, 4, slot)
                if attend and not last:
                    act.wait_ge(s_abs, a + 1)
                    act.activation(buf, buf, ACT.Exp, scale=-1.0).then_inc(s_ex, 1)
                if dense and l in (2, 4):
                    which = l // 2 - 1
                    act.wait_ge(s_read, P * 2 + (R_Q + which + 1))
                    if not (isinstance(P, int) and P < 2):
                        act.wait_ge(s_z, P * 6 - 6)
                    act.activation((qh, kh)[which][:, Pm, :], tmp[:, which, :], ACT.Copy,
                                   scale=(0.125, 1.0)[which]).then_inc(s_qh, 1)
                if attend and not last:
                    act.wait_ge(s_ex, a + 1)
                    act.activation(buf, buf, ACT.Ln, bias=1.0).then_inc(s_ln, 1)
                if attend and not (isinstance(a, int) and (a < 2 or a > NGA + 1)):
                    b = (am - 2) % 12
                    w = GCOLS[b % 3]
                    act.wait_ge(s_tri, a - 1)
                    if not (isinstance(a, int) and a < 4):
                        act.wait_ge(s_pl, a - 3)
                    act.activation(aw[:, b % 2, 0:w], bank[2 + b % 4][:, 0:w], ACT.Exp).then_inc(s_we, 1)

            P_it = [None]

            def block_a(P, Pm, dense, attend):
                for l in range(6):
                    slot_a(P * 6 + (l - 6), (Pm * 6 + l - 6) % 12, P, Pm, l, dense, attend)

            def split_heads(L, p, done):
                act.wait_ge(s_unit, L * U_LAYER + U_O)
                act.wait_ge(s_og, done)
                act.activation(X(ph[0], p), tile(gp, p), ACT.Copy).then_inc(s_oh, 1)

            def out_project(L):
                v = 2 * L + 1

                def body(it):
                    for j in range(4):
                        k = it * 4 + j
                        split_hi_loop(it, L * U_LAYER + U_O + j + 2, 4, (j + 2) % 4)
                        if L == 0:
                            if k > 0:
                                act.wait_ge(s_brow, k)
                            act.activation(toh, oh, ACT.Copy, scale=tb[:, k:k + 1]).then_inc(s_toh, 1)
                        act.wait_ge(s_read, it * 4 + (L * R_LAYER + R_O + j + 1))
                        stream_hi(v, k, gcol(3 + L, k))
                        square(v, k, tile(h, k))
                        if L == 0:
                            act.wait_ge(s_bst, 2 * k + 2)
                            act.dma_start(scratch[k], brow[k % 2]).then_inc(s_bout[k % 2], 16)
                for it in range(2):
                    body(it)

            def embed(L):
                act.wait_ge(s_p, 16 * (L + 1))
                act.activation(psplit[L][0][:, :, :], pstage[L][:, :, :], ACT.Copy).then_inc(s_pfh, 1)

            def embed_gate(L):
                for n in range(4):
                    u = L * U_LAYER + U_P + n
                    split_hi(u + 2, (u + 2) % 4, False)
                norm(2 * L + 1)
                act.preload_act_table(ACT.Sigmoid)
                v = 2 * L + 2
                for n in range(NT):
                    u = L * U_LAYER + U_T + n
                    if u + 2 < UNITS:
                        split_hi(u + 2, (u + 2) % 4, gained(u + 2))
                    act.wait_ge(s_read, L * R_LAYER + R_T + n + 1)
                    act.activation(tmp[:, n % 2, :], tmp[:, n % 2, :], ACT.Sigmoid).then_inc(s_sig, 1)
                    act.wait_ge(s_hg, 8 * L + n + 1)
                    if L == 0:
                        stream_hi(v, n, 1.0)
                    square(v, n, tile(h, n))

            def slot_b(a):
                if a % 4 == 0 and 0 <= a < NSB:
                    hd = a // 4 + 1
                    if 2 <= hd < HEADS_B:
                        act.wait_ge(s_ttr, 8 * (hd - 1))
                        load_bias(hd)
                if 0 <= a < NSB:
                    i = a % 4
                    w = 128 * i + 128
                    act.wait_ge(s_nm, a + 1)
                    c = 8 * (a % 2)
                    act.activation(e1[:, a % 2, 0:w], e1[:, a % 2, 0:w], ACT.Exp, bias=small[:, c + 2:c + 3],
                                   accum_out=small[:, c + 4:c + 5]).then_inc(s_e, 1)
                    act.activation(e2[:, 0:w], e2[:, 0:w], ACT.Exp, bias=small[:, c + 3:c + 4],
                                   accum_out=small[:, c + 5:c + 6]).then_inc(s_e, 1)
                if a >= 5 and (a - 5) % 4 == 0 and (a - 5) // 4 < HEADS_B:
                    hd = (a - 5) // 4
                    act.wait_ge(s_tr, 4 * hd + 4)
                    if hd > 0:
                        act.wait_ge(s_pv, hd)
                    for b, c, w in ((4, 0, 512), (5, 512, 512), (6, 1024, 256)):
                        act.activation(pth[:, c:c + w], bank[b][:, 0:w], ACT.Copy).then_inc(s_pth, 1)
                if a >= 7 and (a - 7) % 4 == 0:
                    hd = (a - 7) // 4
                    act.wait_ge(s_pv, hd + 1)
                    if hd > 0:
                        act.wait_ge(s_nst, hd)
                    act.activation(sq[:, :], bank[7][:, :], ACT.Square).then_inc(s_osq, 1)
                    act.wait_ge(s_nst, hd + 1)
                    if hd > 0:
                        act.wait_ge(s_og, HEADS_A + 1 + hd)
                    act.activation(ssq[:, :], bank[6][:, :], ACT.Ln, scale=1.0 / 128, bias=EPS)\
                       .then_inc(s_nln, 1)
                    act.wait_ge(s_nln, hd + 1)
                    act.activation(ssq[:, :], ssq[:, :], ACT.Exp, scale=-0.5).then_inc(s_nrm, 1)

            def load_bias(hd):
                src = scratch[hd].rearrange("p n -> (p n)")[127:127 + 128 * (BW - 1)]
                act.dma_start(bt[:, hd % 2, :], src.rearrange("(p n) -> p n", n=BW - 1)[:, 0:S])\
                   .then_inc(s_bt[hd % 2], 16)

            def dense_b(P, l):
                if P < 4:
                    if l in (0, 2, 3, 5):
                        c = (0, 2, 3, 5).index(l)
                        u = U_LAYER + U_Q + 4 * P + c + 2
                        split_hi(u, u % 4, gained(u))
                    if l in (2, 3, 5, 6):
                        c = (2, 3, 5, 6).index(l)
                        act.wait_ge(s_read, R_LAYER + R_Q + 4 * P + c + 1)
                        if P >= 2:
                            act.wait_ge(s_s, 16 * (P - 1))
                        act.activation(bqk[c][0][:, P % 2, :], tmp[:, c % 2, :], ACT.Copy,
                                       scale=(1.0, 0.125)[c // 2]).then_inc(s_qh, 1)

            act.dma_start(tmp[:, 0, 0:256], lamp).then_inc(s_lp, 16)
            act.dma_start(sub[:, :], subln).then_inc(s_lp, 16)
            act.wait_ge(s_cst, 16)
            split_hi(0, 0, False)
            for k in range(NT):
                act.wait_ge(s_x[k // 2], 16)
                stream_hi(0, k, gcol(0, k))
                square(0, k, tile(h, k))
            split_hi(1, 1, False)
            gate_project(0)
            values(0)
            act.preload_act_table_set("natural_log_exp_and_others")
            block_a(0, 0, True, False)
            block_a(1, 1, True, True)
            with act.Fori(1, 4) as it:
                P_it[0] = (it, 0)
                block_a(it * 2, 0, True, True)
                P_it[0] = (it, 1)
                block_a(it * 2 + 1, 1, True, True)
            for l in range(6):
                slot_a(42 + l, (42 + l) % 12, 8, 0, l, False, True)
                split_heads(0, l, 2 * l + 3)
            for a in range(NGA, NGA + 2):
                slot_a(a, a % 12, 9, 1, 0, False, True)
            split_heads(0, 6, 15)
            split_heads(0, 7, 17)
            act.wait_ge(s_ol, NT)
            act.dma_start(pstage[0][:, :, :], pT[0].rearrange("k p t -> p k t")).then_inc(s_p, 16)
            act.dma_start(oh, onehot).then_inc(s_tb, 16)
            act.wait_ge(s_tb0, 1)
            act.dma_start(tb[0:NB, :], table).then_inc(s_tb, 16)
            act.wait_ge(s_tb, 32)
            out_project(0)
            embed(0)
            embed_gate(0)
            gate_project(1)
            act.preload_act_table_set("natural_log_exp_and_others")
            for i in range(2):
                act.wait_ge(s_bout[i], 16 * (HEADS_B // 2))
            load_bias(0)
            load_bias(1)
            values(1)
            for P in range(5):
                for l in range(8):
                    slot_b(8 * P + l - 8)
                    dense_b(P, l)
                    if P == 4 and l < 6:
                        split_heads(1, l, HEADS_A + l + 2)
            for a in range(NSB, NSB + 4):
                slot_b(a)
            split_heads(1, 6, HEADS_A + 8)
            split_heads(1, 7, HEADS_A + 9)
            act.wait_ge(s_ol, 2 * NT)
            act.dma_start(pstage[1][:, :, :], pT[1].rearrange("k p t -> p k t")).then_inc(s_p, 16)
            out_project(1)
            embed(1)
            embed_gate(1)
            norm(4)

        @block.vector
        def _(dve):
            def split_lo(u, slot):
                dve.wait_ge(s_wh, u + 1)
                dve.tensor_tensor(wl[:, slot, :], wf[:, slot % 2, :], wh[:, slot, :], ALU.subtract)\
                   .then_inc(s_wl, 1)

            def clear(v):
                if v > 0:
                    dve.wait_ge(s_stat, v)
                dve.memset(ssq[:, :], 0.0).then_inc(s_ss, 1)

            def stream_lo(v, k, gain):
                src, out, hi = tile(h, k), tile(pl[v % 2], k), tile(ph[v % 2], k)
                dve.wait_ge(s_xh, k + (8 * v + 1))
                if gain is None:
                    dve.tensor_tensor(out, src, hi, ALU.subtract).then_inc(s_xl, 1)
                else:
                    dve.scalar_tensor_tensor(out, src, gain, hi, ALU.mult, ALU.subtract).then_inc(s_xl, 1)

            def add_squares(v, k):
                dve.wait_ge(s_sq, k + (8 * v + 1))
                dve.wait_ge(s_ss, k + (9 * v + 1))
                dve.tensor_tensor(ssq[:, :], ssq[:, :], sq[:, :], ALU.add).then_inc(s_ss, 1)

            def scaled(u, r, slot, t):
                dve.wait_ge(s_unit, u + 1)
                dve.tensor_tensor(tmp[:, t, :], bank[slot % 2][:, :], rms[:, :], ALU.mult).then_inc(s_read, 1)

            def gate_project(L):
                for n in range(NT):
                    u, r = L * U_LAYER + U_G + n, L * R_LAYER + R_G + n
                    split_lo(u + 2, (u + 2) % 4)
                    if n == 0:
                        dve.wait_ge(s_rms, 4 * L + 2)
                    if n >= 2:
                        dve.wait_ge(s_silu, NT * L + n - 1)
                    scaled(u, r, n, n % 2)

            def values(L):
                dve.wait_ge(s_silu, NT * (L + 1))
                with dve.Fori(0, 2) as half:
                    for j in range(4):
                        c = L * U_LAYER + U_V + j + 2
                        split_lo(half * 4 + c, (j + 2) % 4)
                    for i in range(4):
                        dst = bass.ds(half * 512 + 1024 * i, 512)
                        dve.wait_ge(s_vh, half * 4 + (8 * L + i + 1))
                        dve.scalar_tensor_tensor(pl[1][:, dst], bank[2 + i][:, :], rmc[:, i:i + 1],
                                                 ph[1][:, dst], ALU.mult, ALU.subtract).then_inc(s_vl, 1)

            def slot_a(a, am, P, Pm, l, dense, attend):
                qh, ql, kh, kl = aqk
                if attend and not (isinstance(a, int) and (a < 1 or a > NGA)):
                    b = (am - 1) % 12
                    w = GCOLS[b % 3]
                    dve.wait_ge(s_lh, a)
                    dve.tensor_tensor(all_[:, b % 4, 0:w], asp[:, b % 2, 0:w], alh[:, b % 4, 0:w],
                                      ALU.subtract).then_inc(s_ll, 1)
                if attend and not (isinstance(a, int) and (a < 6 or a > NGA + 3)) and (am - 6) % 3 == 0:
                    hd = ((am - 6) // 3) % 2
                    head_out(a, hd, P, l)
                if dense and l in (0, 2):
                    split_lo(P * 2 + (U_Q + 2 + l // 2), (2 * Pm + 2 + l // 2) % 4)
                if dense and l in (3, 5):
                    which = (l - 3) // 2
                    dst, hi = (ql, kl)[which], (qh, kh)[which]
                    dve.wait_ge(s_qh, P * 2 + (which + 1))
                    dve.scalar_tensor_tensor(dst[:, Pm, :], tmp[:, which, :], (0.125, 1.0)[which],
                                             hi[:, Pm, :], ALU.mult, ALU.subtract).then_inc(s_qk, 1)
                if dense and l in (2, 4):
                    which = l // 2 - 1
                    scaled(P * 2 + (U_Q + which), None, which, which)
                if attend and not (isinstance(a, int) and a >= NGA):
                    w = GCOLS[am % 3]
                    buf = asp[:, am % 2, 0:w]
                    dve.wait_ge(s_ln, a + 1)
                    dve.scalar_tensor_tensor(buf, bank[2 + am % 4][:, 0:w], 0.0, buf, ALU.max, ALU.add)\
                       .then_inc(s_sp, 1)
                if attend and not (isinstance(a, int) and (a < 2 or a > NGA + 1)):
                    b = (am - 2) % 12
                    w = GCOLS[b % 3]
                    dve.wait_ge(s_mw, a - 1)
                    if not (isinstance(a, int) and a < 4):
                        dve.wait_ge(s_av, a - 3)
                    dve.tensor_copy(awh[:, b % 2, 0:w], aw[:, b % 2, 0:w]).then_inc(s_ph, 1)
                    dve.wait_ge(s_ph, a - 1)
                    dve.tensor_tensor(awl[:, b % 2, 0:w], aw[:, b % 2, 0:w], awh[:, b % 2, 0:w],
                                      ALU.subtract).then_inc(s_pl, 1)

            def head_out(a, hd, P, l):
                p = P - 2
                rows = slice(64 * hd, 64 * hd + 64)
                t = gp[rows, p * S:(p + 1) * S] if isinstance(p, int) else gp[rows, bass.ds(p * S, S)]
                dve.wait_ge(s_av, a - 3)
                dve.tensor_tensor(t, bank[6 + hd][rows, :], t, ALU.mult).then_inc(s_og, 1)

            def block_a(P, Pm, dense, attend):
                for l in range(6):
                    slot_a(P * 6 + (l - 6), (Pm * 6 + l - 6) % 12, P, Pm, l, dense, attend)

            def split_heads(L, p):
                dve.wait_ge(s_oh, NT * L + p + 1)
                dve.tensor_tensor(X(pl[0], p), tile(gp, p), X(ph[0], p), ALU.subtract).then_inc(s_ol, 1)

            def out_project(L):
                v = 2 * L + 1

                def body(it):
                    for j in range(4):
                        c = L * U_LAYER + U_O + j
                        k = it * 4 + j
                        split_lo(it * 4 + (c + 2), (j + 2) % 4)
                        dve.wait_ge(s_unit, it * 4 + (c + 1))
                        dve.tensor_tensor(tile(h, k), tile(h, k), bank[j % 2][:, :], ALU.add).then_inc(s_read, 1)
                        stream_lo(v, k, gcol(3 + L, k))
                        add_squares(v, k)
                        if L == 0:
                            b = 2 + 2 * (k % 2)
                            dve.wait_ge(s_brow, k + 1)
                            if k >= 2:
                                dve.wait_ge(s_bout[k % 2], 16 * (k // 2))
                            dve.tensor_copy(brow[k % 2][:, 0:512], bank[b][:, :]).then_inc(s_bst, 1)
                            dve.tensor_copy(brow[k % 2][:, 512:BW], bank[b + 1][:, 0:BW - 512]).then_inc(s_bst, 1)
                repeat(dve, L == 0, 2, body)

            def embed_gate(L):
                dve.wait_ge(s_pfh, L + 1)
                dve.tensor_tensor(psplit[L][1][:, :, :], pstage[L][:, :, :], psplit[L][0][:, :, :],
                                  ALU.subtract).then_inc(s_pfl, 1)
                if L == 0:
                    for i in range(2):
                        dve.wait_ge(s_bout[i], 16 * (HEADS_B // 2))
                for n in range(4):
                    u = L * U_LAYER + U_P + n
                    split_lo(u + 2, (u + 2) % 4)
                    for nn in range(2):
                        dve.wait_ge(s_ple if nn == 0 else s_unit, 4 * L + n + 1 if nn == 0 else u + 1)
                        dve.tensor_copy(tile(gp, 2 * n + nn), bank[nn][:, :]).then_inc(s_read, 1)
                v = 2 * L + 2
                clear(v)
                dve.wait_ge(s_rms, 2 * (2 * L + 2))
                for n in range(NT):
                    u = L * U_LAYER + U_T + n
                    if u + 2 < UNITS:
                        split_lo(u + 2, (u + 2) % 4)
                    scaled(u, None, n, n % 2)
                    t = tmp[:, n % 2, :]
                    dve.wait_ge(s_sig, NT * L + n + 1)
                    dve.tensor_tensor(t, t, tile(gp, n), ALU.mult).then_inc(s_gm, 1)
                    dve.wait_ge(s_gm, NT * L + n + 1)
                    dve.tensor_tensor(tile(h, n), tile(h, n), t, ALU.add).then_inc(s_hg, 1)
                    if L == 0:
                        stream_lo(v, n, None)
                    add_squares(v, n)

            def combine(a):
                i = a % 4
                w, c = 128 * i + 128, 8 * (a % 2)
                dve.wait_ge(s_e, 2 * a + 2)
                dve.reciprocal(small[:, c + 6:c + 8], small[:, c + 4:c + 6]).then_inc(s_rc, 1)
                dve.wait_ge(s_rc, a + 1)
                dve.tensor_scalar(small[:, c + 7:c + 8], small[:, c + 7:c + 8], lam[:, 3:4], None, ALU.mult)\
                   .then_inc(s_nr, 1)
                dve.tensor_scalar(e1[:, a % 2, 0:w], e1[:, a % 2, 0:w], small[:, c + 6:c + 7], None, ALU.mult)\
                   .then_inc(s_e1n, 1)
                dve.wait_ge(s_nr, a + 1)
                dve.wait_ge(s_e1n, a + 1)
                dve.scalar_tensor_tensor(e1[:, a % 2, 0:w], e2[:, 0:w], small[:, c + 7:c + 8],
                                         e1[:, a % 2, 0:w], ALU.mult, ALU.add).then_inc(s_pr, 1)

            def slot_b(a, P, l):
                if 1 <= a < NSB + 1:
                    combine(a - 1)
                if a >= 6 and (a - 6) % 4 == 0 and (a - 6) // 4 < HEADS_B:
                    hd = (a - 6) // 4
                    for n, (b, c, w) in enumerate(((4, 0, 512), (5, 512, 512), (6, 1024, 256))):
                        dve.wait_ge(s_pth, 3 * hd + n + 1)
                        dve.tensor_tensor(ptl[:, c:c + w], bank[b][:, 0:w], pth[:, c:c + w], ALU.subtract)\
                           .then_inc(s_pte, 1)
                if a >= 8 and a % 4 == 0:
                    hd = (a - 8) // 4
                    dve.wait_ge(s_nrm, hd + 1)
                    dve.tensor_tensor(ssq[:, :], bank[7][:, :], ssq[:, :], ALU.mult).then_inc(s_on, 1)
                if 0 <= a < NSB:
                    hd, i = a // 4, a % 4
                    w, c = 128 * i + 128, 8 * (a % 2)
                    if i == 0:
                        dve.wait_ge(s_bt[hd % 2], 16 * (hd // 2) + 16)
                    if a >= 2:
                        dve.wait_ge(s_tr, a - 1)
                    if a >= 1:
                        dve.wait_ge(s_pr, a)
                    for side, buf in enumerate((e1[:, a % 2, 0:w], e2[:, 0:w])):
                        dve.wait_ge(s_s, 2 * a + side + 1)
                        dve.tensor_tensor_reduce(buf, bank[2 + side][:, 0:w], bt[:, hd % 2, S - w:S], 1.0, -3e38,
                                                 ALU.add, ALU.max, small[:, c + side:c + side + 1])\
                           .then_inc(s_ttr, 1)
                    dve.wait_ge(s_ttr, 2 * a + 2)
                    dve.tensor_scalar(small[:, c + 2:c + 4], small[:, c:c + 2], -1.0, None, ALU.mult)\
                       .then_inc(s_nm, 1)

            def dense_b(P, l):
                if P < 4:
                    if l in (0, 2, 3, 5):
                        u = U_LAYER + U_Q + 4 * P + (0, 2, 3, 5).index(l) + 2
                        split_lo(u, u % 4)
                    if l in (3, 4, 6, 7):
                        c = (3, 4, 6, 7).index(l)
                        dve.wait_ge(s_qh, 2 * (HEADS_A // 2) + 4 * P + c + 1)
                        dve.scalar_tensor_tensor(bqk[c][1][:, P % 2, :], tmp[:, c % 2, :], (1.0, 0.125)[c // 2],
                                                 bqk[c][0][:, P % 2, :], ALU.mult, ALU.subtract)\
                           .then_inc(s_qk, 1)
                    if l in (2, 3, 5, 6):
                        c = (2, 3, 5, 6).index(l)
                        scaled(U_LAYER + U_Q + 4 * P + c, None, c, c % 2)

            dve.memset(tb[NB:NB + 1, :], NEG).then_inc(s_tb0, 1)
            dve.wait_ge(s_trf, 2)
            dve.tensor_scalar(neg1[:, :], ones[:, :], -1.0, None, ALU.mult).then_inc(s_one, 1)
            dve.tensor_copy(tri[:, :], trif[:, :]).then_inc(s_one, 1)
            dve.memset(small[:, 0:8], 0.0).then_inc(s_vl, 1)
            dve.memset(small[:, 8:16], 0.0).then_inc(s_og, 1)
            clear(0)
            dve.wait_ge(s_lp, 32)
            dve.tensor_tensor(lpp, lp[:, 0:4:2, :], lp[:, 1:4:2, :], ALU.mult).then_inc(s_lam, 1)
            dve.wait_ge(s_lam, 1)
            dve.tensor_reduce(lam[:, 0:2], lpp, AX.X, ALU.add).then_inc(s_lam, 1)
            dve.tensor_scalar(sub[:, :], sub[:, :], 1.0 - LAM_INIT, None, ALU.mult).then_inc(s_lam, 1)
            dve.wait_ge(s_cst, 16)
            split_lo(0, 0)
            for k in range(NT):
                stream_lo(0, k, gcol(0, k))
                add_squares(0, k)
            split_lo(1, 1)
            gate_project(0)
            values(0)
            block_a(0, 0, True, False)
            block_a(1, 1, True, True)
            with dve.Fori(1, 4) as it:
                block_a(it * 2, 0, True, True)
                block_a(it * 2 + 1, 1, True, True)
            for l in range(6):
                slot_a(42 + l, (42 + l) % 12, 8, 0, l, False, True)
                split_heads(0, l)
            for a in range(NGA, NGA + 4):
                slot_a(a, a % 12, 9, 1, a - NGA, False, True)
            split_heads(0, 6)
            split_heads(0, 7)
            clear(1)
            out_project(0)
            embed_gate(0)
            gate_project(1)
            dve.wait_ge(s_lame, 1)
            dve.tensor_tensor(lam[:, 2:3], lam[:, 1:2], lam[:, 0:1], ALU.subtract).then_inc(s_lam, 1)
            dve.wait_ge(s_lam, 4)
            dve.tensor_scalar(lam[:, 3:4], lam[:, 2:3], -LAM_INIT, None, ALU.add).then_inc(s_lam, 1)
            values(1)
            dve.wait_ge(s_lam, 5)
            for P in range(5):
                for l in range(8):
                    slot_b(8 * P + l - 8, P, l)
                    dense_b(P, l)
                    if P == 4 and l < 6:
                        split_heads(1, l)
            for a in range(NSB, NSB + 5):
                slot_b(a, 5, a - NSB)
            split_heads(1, 6)
            split_heads(1, 7)
            clear(3)
            out_project(1)
            embed_gate(1)
            dve.wait_ge(s_rms, 10)
            for k in range(NT):
                dve.scalar_tensor_tensor(tile(h, k), tile(h, k), gcol(5, k), rms[:, :], ALU.mult, ALU.mult)\
                   .then_inc(s_fin, 1)

        @block.gpsimd
        def _(pool):
            pool.memset(ones[:, :], 1.0).then_inc(s_trf, 1)
            pool.memset(trif[:, :], -1.0).then_inc(s_t0, 1)
            pool.wait_ge(s_t0, 1)
            pool.affine_select(out=trif[:, :], in_=trif[:, :], compare_op=ALU.is_ge, fill=0.0, base=0,
                               pattern=[[-1, 128]], channel_multiplier=1).then_inc(s_trf, 1)
            pool.wait_ge(s_one, 2)
            pool.memset(trif[:, :], 0.0).then_inc(s_idn, 1)
            pool.wait_ge(s_idn, 1)
            pool.affine_select(out=trif[:, :], in_=trif[:, :], compare_op=ALU.not_equal, fill=1.0, base=0,
                               pattern=[[-1, 128]], channel_multiplier=1).then_inc(s_idn, 1)

            def value_columns(n, slot):
                for src, dst in ((ph[1], vph), (pl[1], vpl)):
                    view = src[:, :].rearrange("p (i c) -> p i c", i=4)
                    pool.tensor_copy(dst[:, slot, :, :], view[:, :, bass.ds(n * 128, 128)]).then_inc(s_vp, 1)

            def diagonal(buf, g):
                n = len(GROUPS[g])
                t = buf[:, 0:128 * n].rearrange("p (b c) -> p b c", b=n)
                return t, n

            def slot_a(a, am, P, Pm, l, copy):
                if l == 3 and copy:
                    if not (isinstance(P, int) and P < 2):
                        pool.wait_ge(s_av, P * 6 - 6)
                    value_columns(P, Pm)
                if isinstance(a, int) and a < 0:
                    return
                if not (isinstance(a, int) and a < 2):
                    pool.wait_ge(s_we, a - 1)
                if not (isinstance(a, int) and a >= NGA):
                    pool.wait_ge(s_sp, a + 1)
                    t, n = diagonal(asp[:, am % 2, :], am % 3)
                    pool.tensor_tensor(t, t, past[:, 0:n, :], ALU.mult).then_inc(s_ml, 1)
                if not (isinstance(a, int) and a < 2):
                    t, n = diagonal(aw[:, am % 2, :], (am - 2) % 3)
                    pool.affine_select(out=t, in_=t, compare_op=ALU.is_gt, fill=0.0, base=0,
                                       pattern=[[0, n], [1, 128]], channel_multiplier=-1).then_inc(s_mw, 1)

            def block_a(P, Pm, copy=True):
                for l in range(6):
                    slot_a(P * 6 + (l - 6), (Pm * 6 + l - 6) % 12, P, Pm, l, copy)

            pool.memset(past[:, :, :], 1.0).then_inc(s_past, 1)
            pool.wait_ge(s_past, 1)
            pool.affine_select(out=past[:, :, :], in_=past[:, :, :], compare_op=ALU.is_gt, fill=0.0, base=0,
                               pattern=[[0, 2], [1, 128]], channel_multiplier=-1).then_inc(s_past, 1)
            pool.wait_ge(s_past, 2)
            pool.wait_ge(s_vl, 9)
            block_a(0, 0)
            block_a(1, 1)
            with pool.Fori(1, 4) as it:
                block_a(it * 2, 0)
                block_a(it * 2 + 1, 1)
            block_a(8, 0, False)
            for a in range(NGA, NGA + 2):
                slot_a(a, a % 12, 9, 1, 1, False)

            def gain(u, g, per):
                k0 = 0 if per == 128 else 2 * (u % 4)
                t = wf[:, u % 2, :].rearrange("p (k c) -> p k c", c=per)
                n = UNIT // per
                pool.wait_ge(s_wd[u % 2], 16 * (u // 2) + 16)
                col = gn[:, g * NT + k0:g * NT + k0 + n].rearrange("p (k o) -> p k o", o=1).to_broadcast([128, n, per])
                pool.tensor_tensor(t, t, col, ALU.mult).then_inc(s_wg, 1)

            def gate_head(a):
                hd = (a - 8) // 4
                pool.wait_ge(s_on, hd + 1)
                pool.tensor_tensor(tile(gp, hd), ssq[:, :], tile(gp, hd), ALU.mult).then_inc(s_og, 1)

            for n in range(U_V):
                gain(U_LAYER + U_G + n, 2, 128)
            for n in range(U_Q - U_V):
                gain(U_LAYER + U_V + n, 1, 512)
                if n < 4:
                    for m in range(2 * n, 2 * n + 2):
                        pool.wait_ge(s_silu, NT + m + 1)
                        if m == 0:
                            pool.wait_ge(s_lam, 3)
                        pool.tensor_scalar(tile(gp, m), tile(gp, m), sub[:, 0:1], None, ALU.mult).then_inc(s_silc, 1)
            q_units = [(U_LAYER + U_Q + n, 1 if n % 4 < 2 else 2) for n in range(16)]
            for n in range(2):
                gain(*q_units.pop(0), 128)
            pool.wait_ge(s_vl, 17)
            for hd in range(2):
                value_columns(hd, hd)
            for P in range(5):
                for l in range(8):
                    a = 8 * P + l - 8
                    if a >= 8 and a % 4 == 0:
                        pool.wait_ge(s_pv, a // 4 - 1)
                        value_columns(a // 4, (a // 4) % 2)
                    if P < 4 and l in (0, 2, 3, 5) and q_units:
                        gain(*q_units.pop(0), 128)
                    if a >= 8 and a % 4 == 0:
                        gate_head(a)
            for a in range(NSB, NSB + 5):
                if a % 4 == 0:
                    gate_head(a)


def bucket_rows():
    dist = 511 - np.arange(BW)
    n = np.maximum(dist, 0)
    nf = np.maximum(n, 1).astype(np.float32)
    half = NB // 2
    large = half + (np.log(nf / half) / np.float32(math.log(128 / half)) * (NB - half)).astype(np.int32)
    b = np.where(n < half, n, np.minimum(large, NB - 1))
    rows = np.zeros((NB + 1, BW), np.float32)
    for j in range(BW):
        rows[b[j] if dist[j] >= 0 else NB, j] = 1.0
    return rows


def kernel(x, p, attn_norm, w_in_a, w_out_a, kv_norm, w_kv, w_q_b, diff_lambda, diff_subln, w_out_b,
           rel_bias, ple_norm, w_ple_proj, w_ple_gate, final_norm):
    import concourse.bacc as _bacc
    from concourse.bass_utils import run_bass_kernel_spmd as _run

    def cols(w):
        k, n = w.shape
        return w.reshape(k // 128, 128, n // 128, 128).transpose(2, 1, 0, 3).reshape(n // 128, 128, -1)

    def slabs(w):
        return w.reshape(4, 2, 128, w.shape[1] // 512, 512).transpose(3, 0, 2, 1, 4).reshape(-1, 128, UNIT)

    def pairs(w):
        u = cols(w).reshape(4, 2, 128, 256).transpose(0, 2, 1, 3).reshape(4, 128, 512)
        return np.concatenate([u, np.zeros_like(u)], axis=2)

    def woven(*parts):
        return np.stack(parts, axis=1).reshape(-1, 128, UNIT)

    w_in, w_oa, w_qb, w_ob = w_in_a[0], w_out_a[0], w_q_b[0], w_out_b[0]
    units = np.concatenate([
        cols(w_in[:, 3 * D:]), slabs(w_in[:, 2 * D:3 * D]),
        woven(cols(w_in[:, :D]), cols(w_in[:, D:2 * D])),
        cols(w_oa), pairs(w_ple_proj[0]), cols(w_ple_gate[0]),
        cols(w_qb[:, D:]), slabs(w_kv[:, D:]),
        woven(cols(w_kv[:, :512]), cols(w_kv[:, 512:D]), cols(w_qb[:, :512]), cols(w_qb[:, 512:D])),
        cols(w_ob), pairs(w_ple_proj[1]), cols(w_ple_gate[1])])
    gains = np.stack([attn_norm[0], kv_norm, attn_norm[1], ple_norm[0], ple_norm[1], final_norm])
    arrays = {
        "xT": x[0].T.reshape(NT, 128, S),
        "pT": p[:, 0].transpose(0, 2, 1).reshape(2, DP // 128, 128, S),
        "w_units": units,
        "gains": gains.reshape(6, NT, 128).transpose(2, 0, 1).reshape(128, 6 * NT),
        "subln": diff_subln.reshape(128, 1),
        "lamp": np.broadcast_to(diff_lambda.reshape(1, 256), (128, 256)),
        "table": rel_bias,
        "onehot": bucket_rows(),
    }
    arrays = {f"in_{n}": np.ascontiguousarray(v) for n, v in arrays.items()}
    nc = _bacc.Bacc("TRN2", target_bir_lowering=False, num_devices=1)
    ins = [nc.dram_tensor(n, v.shape, F32, kind="ExternalInput").ap() for n, v in arrays.items()]
    scratch = nc.dram_tensor("bias_rows", (HEADS_B, 128, BW), F32, kind="Internal").ap()
    outT = nc.dram_tensor("outT", (NT, 128, S), F32, kind="ExternalOutput").ap()
    build(nc, *ins, scratch, outT)
    got = _run(nc, [arrays], core_ids=[0]).results[0]["outT"]
    return np.ascontiguousarray(got.reshape(D, S).T).reshape(1, S, D)
```

```python
from contextlib import ExitStack
import math

import numpy as np
import concourse.bass as bass
from concourse import mybir

F32 = mybir.dt.float32
F32R = mybir.dt.float32r
ALU = mybir.AluOpType
ACT = mybir.ActivationFunctionType
AX = mybir.AxisListType

D = 1024
S = 512
NT = D // 128
DP = 256
HEADS_A = 16
HEADS_B = 8
NB = 32
EPS = 1e-6
LAM_INIT = 0.8 - 0.6 * math.exp(-0.3 * 1)
NEG = -1e30
UNIT = 1024

U_G, U_V, U_Q, U_O, U_P, U_T, U_LAYER = 0, 8, 16, 32, 40, 44, 52
R_G, R_Q, R_O, R_P, R_T, R_LAYER = 0, 8, 24, 32, 40, 48
UNITS = 2 * U_LAYER

BW = 640
GROUPS = [[(3, 0), (2, 128)], [(1, 0)], [(0, 0)]]
GCOLS = [384, 384, 512]
NGA = 3 * HEADS_A
NSB = 4 * HEADS_B
Q_TILES = [0, 5, 10, 16, 21, 26, 30, 32, 32]
Q_READ, Q_HI, Q_LO, Q_WEIGHTS = (2, 3, 5, 6.5), (2.5, 3.5, 5.5, 7), (3, 4, 6, 7.5), (0, 2, 3, 5)
COPIES = [(6, 1024, 256), (5, 512, 512), (4, 0, 512)]


def build(nc, xT, pT, w_units, gains, subln, lamp, table, onehot, scratch, outT):
    with ExitStack() as ctx:
        def sb(name, shape, dt=F32, where=ctx):
            return where.enter_context(nc.sbuf_tensor(name, shape, dt))

        def sem(name):
            return ctx.enter_context(nc.semaphore(name))

        bank = [ctx.enter_context(nc.psum_tensor(f"bank{i}", [128, 512], F32)) for i in range(8)]

        h = sb("h", [128, NT * S])
        ph = [sb(f"split{i}_hi", [128, NT * S], F32R) for i in range(2)]
        pl = [sb(f"split{i}_lo", [128, NT * S], F32R) for i in range(2)]
        gp = sb("gp", [128, NT * S])
        wf = sb("w_f32", [128, 2, UNIT])
        wh = sb("w_hi", [128, 4, UNIT], F32R)
        wl = sb("w_lo", [128, 4, UNIT], F32R)
        rms = sb("rms", [128, S])
        rmc = sb("rms_col", [128, 4])
        ssq = sb("ssq", [128, S])
        sq = sb("sq", [128, S])
        tmp = sb("tmp", [128, 2, S])
        ones = sb("ones", [128, 128])
        trif = sb("trif", [128, 128])
        gn = sb("gains_sb", [128, 6 * NT])
        sub = sb("subln_sb", [128, 1])
        lp = tmp[:, 0, 0:256].rearrange("p (a d) -> p a d", a=4)
        lpp = tmp[:, 1, 0:128].rearrange("p (a d) -> p a d", a=2)
        lam = sb("lam", [128, 4])
        tb = sb("table_sb", [NB + 1, HEADS_B])
        small = sb("small", [128, 16])

        tA, tB = ExitStack(), ExitStack()
        with tA:
            vph = sb("v_cols_hi", [128, 2, 4, 128], F32R, tA)
            vpl = sb("v_cols_lo", [128, 2, 4, 128], F32R, tA)
            neg1 = sb("neg1", [128, 128], F32R, tA)
            future = sb("future", [128, 128], F32R, tA)
            idr = sb("identity_r", [128, 128], F32R, tA)
            tri = sb("tri", [128, 128], F32R, tA)
            asp = sb("sp", [128, 2, S], F32, tA)
            aw = sb("w_att", [128, 2, S], F32, tA)
            alh = sb("l_hi", [128, 4, S], F32R, tA)
            all_ = sb("l_lo", [128, 4, S], F32R, tA)
            awh = sb("wa_hi", [128, 2, S], F32R, tA)
            awl = sb("wa_lo", [128, 2, S], F32R, tA)
            aqk = [sb(n, [128, 2, S], F32R, tA) for n in ("a_qh", "a_ql", "a_kh", "a_kl")]
        with tB:
            e1 = sb("e1", [128, 4, S], F32, tB)
            e2 = sb("e2", [128, 2, S], F32, tB)
            bt = sb("bias_tile", [128, 2, S], F32, tB)
            pth = sb("pt_hi", [128, 1280], F32R, tB)
            ptl = sb("pt_lo", [128, 1280], F32R, tB)
            bqk = [[sb(f"b_{n}{q}", [128, 2, S], F32R, tB) for q in "hl"] for n in ("k1", "k2", "q1", "q2")]
        pstage = [asp, e2]
        psplit = [(aqk[0], aqk[1]), (bqk[0][0], bqk[0][1])]
        oh = gp[0:NB + 1, 0:BW]
        toh = gp[0:NB + 1, 1024:1024 + BW]
        brow = [gp[:, 2048:2048 + BW], gp[:, 3072:3072 + BW]]

        s_x = [sem(f"s_x{i}") for i in range(4)]
        s_cst = sem("s_cst")
        s_lp = sem("s_lp")
        s_tb = sem("s_tb")
        s_wd = [sem(f"s_wd{i}") for i in range(2)]
        s_wg = sem("s_wg")
        s_wh = sem("s_wh")
        s_wl = sem("s_wl")
        s_one = sem("s_one")
        s_trf = sem("s_trf")
        s_idn = sem("s_idn")
        s_unit = sem("s_unit")
        s_ple = sem("s_ple")
        s_read = sem("s_read")
        s_vres = sem("s_vres")
        s_vh = sem("s_vh")
        s_vl = sem("s_vl")
        s_xh = sem("s_xh")
        s_xl = sem("s_xl")
        s_sq = sem("s_sq")
        s_ss = sem("s_ss")
        s_stat = sem("s_stat")
        s_lnr = sem("s_lnr")
        s_rms = sem("s_rms")
        s_silu = sem("s_silu")
        s_silc = sem("s_silc")
        s_qh = sem("s_qh")
        s_qk = sem("s_qk")
        s_z = sem("s_z")
        s_abs = sem("s_abs")
        s_ex = sem("s_ex")
        s_ln = sem("s_ln")
        s_sp = sem("s_sp")
        s_lh = sem("s_lh")
        s_ll = sem("s_ll")
        s_tri = sem("s_tri")
        s_we = sem("s_we")
        s_ph = sem("s_ph")
        s_pl = sem("s_pl")
        s_av = sem("s_av")
        s_vp = sem("s_vp")
        s_og = sem("s_og")
        s_oh = sem("s_oh")
        s_ol = sem("s_ol")
        s_toh = sem("s_toh")
        s_brow = sem("s_brow")
        s_bst = sem("s_bst")
        s_bout = [sem(f"s_bout{i}") for i in range(2)]
        s_t0 = sem("s_t0")
        s_tb0 = sem("s_tb0")
        s_p = sem("s_p")
        s_pfh = sem("s_pfh")
        s_pfl = sem("s_pfl")
        s_sig = sem("s_sig")
        s_gm = sem("s_gm")
        s_hg = sem("s_hg")
        s_lam = sem("s_lam")
        s_lame = sem("s_lame")
        s_bt = [sem(f"s_bt{i}") for i in range(2)]
        s_s = sem("s_s")
        s_ttr = sem("s_ttr")
        s_nm = sem("s_nm")
        s_e = sem("s_e")
        s_rc = sem("s_rc")
        s_nr = sem("s_nr")
        s_e1n = sem("s_e1n")
        s_pr = sem("s_pr")
        s_tr = sem("s_tr")
        s_pth = sem("s_pth")
        s_pte = sem("s_pte")
        s_pv = sem("s_pv")
        s_osq = sem("s_osq")
        s_nst = sem("s_nst")
        s_nln = sem("s_nln")
        s_nrm = sem("s_nrm")
        s_on = sem("s_on")
        s_fin = sem("s_fin")
        s_out = sem("s_out")

        def X(which, k, part=slice(0, S)):
            return which[:, k * S + part.start:k * S + part.stop]

        def tile(buf, k):
            return buf[:, k * S:(k + 1) * S] if isinstance(k, int) else buf[:, bass.ds(k * S, S)]

        def gcol(g, k):
            return gn[:, g * NT + k:g * NT + k + 1] if isinstance(k, int) else gn[:, bass.ds(k + g * NT, 1)]

        def repeat(eng, unrolled, n, body):
            if unrolled:
                for it in range(n):
                    body(it)
            else:
                with eng.Fori(0, n) as it:
                    body(it)

        def gained(u):
            return u >= U_LAYER and u < U_LAYER + U_O

        block = ctx.enter_context(nc.Block())

        @block.sync
        def _(sp):
            sp.dma_start(gn[:, :], gains).then_inc(s_cst, 16)
            sp.dma_start(wf[:, 0, :], w_units[0]).then_inc(s_wd[0], 16)
            for i in range(4):
                sp.dma_start(h[:, 2 * i * S:(2 * i + 2) * S].rearrange("p (k t) -> p k t", k=2),
                             xT[2 * i:2 * i + 2].rearrange("k p t -> p k t")).then_inc(s_x[i], 16)
                if i == 0:
                    sp.dma_start(wf[:, 1, :], w_units[1]).then_inc(s_wd[1], 16)
            with sp.Fori(1, UNITS // 2) as i:
                for slot in range(2):
                    sp.wait_ge(s_wl, i * 2 + (slot - 1))
                    sp.dma_start(wf[:, slot:slot + 1, :],
                                 w_units.rearrange("u p n -> p u n")[:, bass.ds(i * 2 + slot, 1), :]).then_inc(s_wd[slot], 16)
            for k in range(NT):
                sp.wait_ge(s_fin, k + 1)
                sp.dma_start(outT[k], tile(h, k)).then_inc(s_out, 16)
            sp.wait_ge(s_out, 16 * NT)
            for i in range(2):
                sp.wait_ge(s_bout[i], 16 * (HEADS_B // 2))

        @block.tensor
        def _(pe):
            def mm3(out, lh, ll, rh, rl, start, stop, last=None):
                pe.matmul(out, lhsT=lh, rhs=rh, start=start, stop=False, skip_group_check=True)
                pe.matmul(out, lhsT=lh, rhs=rl, start=False, stop=False, skip_group_check=True)
                return pe.matmul(out, lhsT=ll, rhs=rh, start=False, stop=stop, skip_group_check=True)

            def product(slot, which, k, start, stop):
                c = slice(128 * k, 128 * k + 128)
                return mm3(bank[slot % 2][:, :], wh[:, slot, c], wl[:, slot, c],
                           X(ph[which], k), X(pl[which], k), start, stop)

            def open_unit(u, slot, r):
                pe.wait_ge(s_wl, u + 1)
                if not isinstance(r, int) or r >= 2:
                    pe.wait_ge(s_read, r - 1)

            def unit(u, slot, which, r, ready=None):
                open_unit(u, slot, r)
                for k in range(NT):
                    if ready is not None:
                        pe.wait_ge(ready[0], ready[1] + k + 1)
                    last = product(slot, which, k, k == 0, k == NT - 1)
                last.then_inc(s_unit, 1)

            def stat(v):
                pe.wait_ge(s_ss, 9 * (v + 1))
                pe.matmul(bank[6][:, :], lhsT=ones[:, :], rhs=ssq[:, :], start=True, stop=True)
                for i in range(4):
                    last = pe.matmul(bank[7][:, i:i + 1], lhsT=ssq[:, 128 * i:128 * i + 128],
                                     rhs=ones[:, 0:1], start=(i == 0), stop=True, skip_group_check=True)
                last.then_inc(s_stat, 1)

            def values(L):
                with pe.Fori(0, 2) as half:
                    pe.wait_ge(s_vl, half * 4 + (8 * L + 1))
                    for j in range(4):
                        pe.wait_ge(s_wl, half * 4 + (L * U_LAYER + U_V + j + 1))
                        for i in range(4):
                            rows = slice(128 * i, 128 * i + 128)
                            for kk in range(2):
                                k = 2 * j + kk
                                c = slice(512 * kk, 512 * kk + 512)
                                last = mm3(bank[2 + i][:, :], X(ph[0], k, rows), X(pl[0], k, rows),
                                           wh[:, j, c], wl[:, j, c], k == 0, k == NT - 1)
                            if j == 3 and i < 3:
                                last.then_inc(s_vres, 1)
                        last.then_inc(s_unit, 1)

            def scores_a(a, am, P):
                g, hd = am % 3, (am // 3) % 2
                z = bank[2 + am % 4]
                par = (am // 6 + 0) % 2
                if am % 6 == 0:
                    pe.wait_ge(s_qk, P * 2)
                if not isinstance(a, int) or a >= 4:
                    pe.wait_ge(s_we, a - 3)
                qh, ql, kh, kl = aqk
                rows = slice(64 * hd, 64 * hd + 64)
                for n, (i, off) in enumerate(GROUPS[g]):
                    w = S - 128 * i
                    o = z[:, off:off + w]
                    kc, qc = slice(128 * i, 128 * i + 128), slice(128 * i, S)
                    last = mm3(o, kh[rows, par, kc], kl[rows, par, kc], qh[rows, par, qc], ql[rows, par, qc],
                               n == 0, True)
                    last = pe.matmul(z[:, off:off + 128], lhsT=idr[:, :], rhs=future[:, :], start=False, stop=True,
                                     skip_group_check=True)
                last.then_inc(s_z, 1)

            def logsums(a, am):
                g = am % 3
                z = bank[2 + am % 4]
                pe.wait_ge(s_ll, a + 1)
                for i, off in GROUPS[g]:
                    for j in range(i, 4):
                        gj = 2 - j if j < 2 else 0
                        slot = (am - g + gj) % 4
                        src = dict(GROUPS[gj])[j]
                        w = S - 128 * j
                        o = z[:, off + 128 * (j - i):off + 128 * (j - i) + w]
                        st = tri if j == i else neg1
                        for part in (alh, all_):
                            last = pe.matmul(o, lhsT=st[:, :], rhs=part[:, slot, src:src + w], start=False,
                                             stop=True, skip_group_check=True)
                last.then_inc(s_tri, 1)

            def heads_a(a, am, P):
                g, hd = am % 3, (am // 3) % 2
                par = (am // 6) % 2
                o = bank[6 + hd]
                pe.wait_ge(s_pl, a + 1)
                if g == 0:
                    if hd == 0:
                        pe.wait_ge(s_vp, P * 2)
                    pe.wait_ge(s_og, P * 2 + (hd - 2))
                for i, off in GROUPS[g]:
                    w = S - 128 * i
                    last = mm3(o[:, 128 * i:S], vph[:, par, i, :], vpl[:, par, i, :],
                               awh[:, am % 2, off:off + w], awl[:, am % 2, off:off + w], i == 3, True)
                last.then_inc(s_av, 1)

            def block_a(P, Pm, dense, attend):
                a0 = P * 6 - 6 if isinstance(P, int) else P * 6 + (-6)
                u0 = P * 2 + U_Q
                for l in range(6):
                    am = (Pm * 6 + l - 6) % 12
                    a = a0 + l
                    if attend:
                        scores_a(a, am, P)
                    if attend and not (isinstance(a, int) and a < 2):
                        logsums(a - 2, (am - 2) % 12)
                    if dense and l < 4:
                        c = l // 2
                        slot = (2 * Pm + c) % 4
                        if l % 2 == 0:
                            open_unit(u0 + c, slot, P * 2 + (R_Q + c))
                        for k in range(4 * (l % 2), 4 * (l % 2) + 4):
                            last = product(slot, 0, k, k == 0, k == NT - 1)
                        if l % 2:
                            last.then_inc(s_unit, 1)
                    if not dense and l > 0:
                        out_early(0, l - 1)
                    if attend and not (isinstance(a, int) and a < 3):
                        heads_a(a - 3, (am - 3) % 12, P if l >= 3 else P - 1)

            def tiles(L, U, R, which, ready):
                with pe.Fori(0, 2) as it:
                    for j in range(4):
                        unit(it * 4 + (L * U_LAYER + U + j), j, which, it * 4 + (L * R_LAYER + R + j),
                             ready if j == 0 else None)

            def out_early(L, k):
                for c in range(2):
                    if k == 0:
                        open_unit(L * U_LAYER + U_O + c, c, L * R_LAYER + R_O + c)
                    pe.wait_ge(s_ol, NT * L + k + 1)
                    product(c, 0, k, k == 0, False)

            def bias_row(hd):
                b = 2 + 2 * (hd % 2)
                pe.wait_ge(s_toh, hd + 1)
                if hd >= 2:
                    pe.wait_ge(s_bst, 2 * hd - 2)
                pe.matmul(bank[b][:, :], lhsT=ones[0:NB + 1, :], rhs=toh[:, 0:512], start=True, stop=True)
                pe.matmul(bank[b + 1][:, 0:BW - 512], lhsT=ones[0:NB + 1, :], rhs=toh[:, 512:BW],
                          start=True, stop=True).then_inc(s_brow, 1)

            def scores_b(a, P):
                i = 3 - a % 4
                hd = a // 4
                if a % 8 == 0:
                    pe.wait_ge(s_qk, 2 * HEADS_A // 2 + 4 * P)
                rows = slice(64 * (hd % 2), 64 * (hd % 2) + 64)
                par = (P - 1) % 2
                w = 128 * i + 128
                qc = slice(128 * i, 128 * i + 128)
                for side in range(2):
                    kh, kl = bqk[side]
                    qh, ql = bqk[2 + side]
                    if a >= 1:
                        pe.wait_ge(s_ttr, 2 * a - 1 + side)
                    mm3(bank[2 + side][:, 0:w], qh[rows, par, qc], ql[rows, par, qc],
                        kh[rows, par, 0:w], kl[rows, par, 0:w], True, True).then_inc(s_s, 1)

            PT = [(4, 0, 0, 2), (5, 0, 512, 1), (6, 0, 1024, 0), (5, 384, 896, 1)]

            def transposes(a):
                hd, i = a // 4, 3 - a % 4
                pe.wait_ge(s_pr, a + 1)
                for j in (2, 3, 1, 0):
                    if j > i:
                        continue
                    b, c, _, copy = PT[j]
                    if i == 3:
                        if hd > 0:
                            pe.wait_ge(s_pte, 3 * hd - 2 + copy)
                        if j == 2 and hd > 1:
                            pe.wait_ge(s_nln, hd - 1)
                    c += 128 * (i - j)
                    last = pe.transpose(bank[b][:, c:c + 128], e1[:, a % 4, 128 * j:128 * j + 128], trif[:, :])
                last.then_inc(s_tr, 1)

            def head_b(hd):
                if hd > 0:
                    pe.wait_ge(s_on, hd)
                for j in (2, 3, 1, 0):
                    w = S - 128 * j
                    _, _, c, copy = PT[j]
                    pe.wait_ge(s_pte, 3 * hd + 1 + copy)
                    v = slice(UNIT * j + 128 * hd, UNIT * j + 128 * hd + 128)
                    last = mm3(bank[7][:, 128 * j:S], ph[1][:, v], pl[1][:, v],
                               pth[:, c:c + w], ptl[:, c:c + w], j == 2, True)
                last.then_inc(s_pv, 1)

            def head_stat(hd):
                pe.wait_ge(s_osq, hd + 1)
                if hd < HEADS_B - 1:
                    pe.wait_ge(s_pte, 3 * hd + 4)
                pe.matmul(bank[6][:, :], lhsT=ones[:, :], rhs=sq[:, :], start=True, stop=True).then_inc(s_nst, 1)

            def block_b(P):
                for l in range(8):
                    a = 8 * P + l - 8
                    if 0 <= a < NSB:
                        scores_b(a, P)
                    if P == 4 and 1 <= l < 6:
                        out_early(1, l - 1)
                    if P < 4:
                        for m in range(Q_TILES[l], Q_TILES[l + 1]):
                            c, k = m // 8, m % 8
                            if k == 0:
                                open_unit(U_LAYER + U_Q + 4 * P + c, c, R_LAYER + R_Q + 4 * P + c)
                            last = product(c, 0, k, k == 0, k == NT - 1)
                            if k == NT - 1:
                                last.then_inc(s_unit, 1)
                    tail_b(a)

            def tail_b(a):
                if a >= 6 and (a - 6) % 4 == 0 and (a - 6) // 4 < HEADS_B:
                    head_b((a - 6) // 4)
                if 2 <= a < NSB + 2:
                    transposes(a - 2)
                if a >= 8 and a % 4 == 0:
                    head_stat((a - 8) // 4)

            def gate_project(L):
                v = 2 * L
                for k, c in [(0, 0), (1, 0), (0, 1), (1, 1)] + [(k, c) for k in range(2, NT) for c in range(2)]:
                    if k == 0:
                        open_unit(L * U_LAYER + U_G + c, c, L * R_LAYER + R_G + c)
                    pe.wait_ge(s_xl, 8 * v + k + 1)
                    last = product(c, 0, k, k == 0, k == NT - 1)
                    if k == NT - 1:
                        last.then_inc(s_unit, 1)
                stat(v)
                for n in range(2, NT):
                    unit(L * U_LAYER + U_G + n, n % 4, 0, L * R_LAYER + R_G + n)

            def rest(L):
                base = L * U_LAYER
                for n in range(NT):
                    if n < 2:
                        for k in range(6, NT):
                            pe.wait_ge(s_ol, NT * L + k + 1)
                            last = product(n, 0, k, False, k == NT - 1)
                        last.then_inc(s_unit, 1)
                    else:
                        unit(base + U_O + n, n % 4, 0, L * R_LAYER + R_O + n)
                    if L == 0:
                        bias_row(n)
                pe.wait_ge(s_pfl, L + 1)
                fh, fl = psplit[L]
                for n in range(4):
                    pe.wait_ge(s_wl, base + U_P + n + 1)
                    for nn in range(2):
                        pe.wait_ge(s_read, L * R_LAYER + R_P + 2 * n + nn - 1)
                        for kk in range(2):
                            c = slice(128 * (2 * nn + kk), 128 * (2 * nn + kk) + 128)
                            last = mm3(bank[nn][:, :], wh[:, n, c], wl[:, n, c], fh[:, kk, :], fl[:, kk, :],
                                       kk == 0, kk == 1)
                        last.then_inc(s_ple if nn == 0 else s_unit, 1)
                stat(2 * L + 1)
                tiles(L, U_T, R_T, 1, (s_xl, 8 * (2 * L + 1)))

            gate_project(0)
            values(0)
            pe.wait_ge(s_one, 4)
            block_a(0, 0, True, False)
            block_a(1, 1, True, True)
            with pe.Fori(1, 4) as it:
                block_a(it * 2, 0, True, True)
                block_a(it * 2 + 1, 1, True, True)
            block_a(8, 0, False, True)
            for a in range(NGA, NGA + 3):
                if a == NGA + 1:
                    out_early(0, 5)
                if a < NGA + 2:
                    logsums(a - 2, (a - 2) % 12)
                heads_a(a - 3, (a - 3) % 12, 8)
            rest(0)
            gate_project(1)
            values(1)
            pe.wait_ge(s_idn, 2)
            for P in range(5):
                block_b(P)
            for a in range(NSB, NSB + 5):
                if a == NSB + 1:
                    out_early(1, 5)
                tail_b(a)
            rest(1)
            stat(4)

        @block.scalar
        def _(act):
            def split_hi(u, slot, gain):
                if gain:
                    act.wait_ge(s_wg, u + (1 - U_LAYER))
                elif isinstance(u, int):
                    act.wait_ge(s_wd[slot % 2], 16 * (u // 2) + 16)
                act.wait_ge(s_unit, u - 3) if not isinstance(u, int) or u > 3 else None
                act.activation(wh[:, slot, :], wf[:, slot % 2, :], ACT.Copy).then_inc(s_wh, 1)

            def split_hi_loop(it, c, step, slot):
                act.wait_ge(s_wd[slot % 2], it * (8 * step) + (16 * (c // 2) + 16))
                act.wait_ge(s_unit, it * step + (c - 3))
                act.activation(wh[:, slot, :], wf[:, slot % 2, :], ACT.Copy).then_inc(s_wh, 1)

            def square(v, k, src):
                act.wait_ge(s_ss, k + (9 * v + 1))
                act.activation(sq[:, :], src, ACT.Square).then_inc(s_sq, 1)

            def norm(v):
                act.preload_act_table_set("natural_log_exp_and_others")
                act.wait_ge(s_stat, v + 1)
                act.activation(rms[:, :], bank[6][:, :], ACT.Ln, scale=1.0 / D, bias=EPS).then_inc(s_lnr, 1)
                act.activation(rmc[:, :], bank[7][:, 0:4], ACT.Ln, scale=1.0 / D, bias=EPS).then_inc(s_lnr, 1)
                act.wait_ge(s_lnr, 2 * v + 2)
                act.activation(rms[:, :], rms[:, :], ACT.Exp, scale=-0.5).then_inc(s_rms, 1)
                act.activation(rmc[:, :], rmc[:, :], ACT.Exp, scale=-0.5).then_inc(s_rms, 1)

            def gate_project(L):
                for n in range(NT):
                    u = L * U_LAYER + U_G + n
                    split_hi(u + 2, (u + 2) % 4, gained(u + 2))
                    if n == 0:
                        norm(2 * L)
                        if L == 0:
                            act.wait_ge(s_lam, 3)
                            act.activation(lam[:, 0:2], lam[:, 0:2], ACT.Exp).then_inc(s_lame, 1)
                        act.preload_act_table(ACT.Silu)
                    act.wait_ge(s_read, L * R_LAYER + R_G + n + 1)
                    if L == 1 and n == 0:
                        act.wait_ge(s_hg, NT)
                    act.activation(tile(gp, n), tmp[:, n % 2, :], ACT.Silu).then_inc(s_silu, 1)

            def values(L):
                act.wait_ge(s_rms, 4 * L + 2)
                for half in range(2):
                    for j in range(4):
                        c = L * U_LAYER + U_V + j + 2
                        slot = (j + 2) % 4
                        if L == 1:
                            act.wait_ge(s_wg, half * 4 + (c + 1 - U_LAYER))
                            act.wait_ge(s_unit, half * 4 + (c - 3))
                            act.activation(wh[:, slot, :], wf[:, slot % 2, :], ACT.Copy).then_inc(s_wh, 1)
                        else:
                            split_hi_loop(half, c, 4, slot)
                    for i in range(4):
                        if i < 3:
                            act.wait_ge(s_vres, half * 3 + (6 * L + i + 1))
                        else:
                            act.wait_ge(s_unit, half * 4 + (L * U_LAYER + U_V + 4))
                        act.activation(ph[1][:, 1024 * i + 512 * half:1024 * i + 512 * half + 512], bank[2 + i][:, :], ACT.Copy,
                                       scale=rmc[:, i:i + 1]).then_inc(s_vh, 1)

            def stream_hi(v, k, scale):
                act.activation(tile(ph[v % 2], k), tile(h, k), ACT.Copy, scale=scale).then_inc(s_xh, 1)

            def slot_a(a, am, P, Pm, l, dense, attend):
                qh, ql, kh, kl = aqk
                last = isinstance(a, int) and a >= NGA
                if attend and not last:
                    w = GCOLS[am % 3]
                    buf = asp[:, am % 2, 0:w]
                    act.wait_ge(s_z, a + 1)
                    if not (isinstance(a, int) and a < 2):
                        act.wait_ge(s_ll, a - 1)
                    act.activation(buf, bank[2 + am % 4][:, 0:w], ACT.Abs).then_inc(s_abs, 1)
                if attend and not (isinstance(a, int) and (a < 1 or a > NGA)):
                    b = (am - 1) % 12
                    act.wait_ge(s_sp, a)
                    if not (isinstance(a, int) and a < 3):
                        act.wait_ge(s_tri, a - 2)
                    act.activation(alh[:, b % 4, 0:GCOLS[b % 3]], asp[:, b % 2, 0:GCOLS[b % 3]],
                                   ACT.Copy).then_inc(s_lh, 1)
                if attend and not (isinstance(a, int) and (a < 2 or a > NGA + 1)):
                    b = (am - 2) % 12
                    w = GCOLS[b % 3]
                    act.wait_ge(s_tri, a - 1)
                    if not (isinstance(a, int) and a < 4):
                        act.wait_ge(s_pl, a - 3)
                    act.activation(aw[:, b % 2, 0:w], bank[2 + b % 4][:, 0:w], ACT.Exp).then_inc(s_we, 1)
                if dense and l in (0, 2):
                    c = U_Q + 2 + l // 2
                    slot = (2 * Pm + 2 + l // 2) % 4
                    if isinstance(P, int):
                        split_hi(2 * P + c, slot, False)
                    else:
                        it, b = P_it[0]
                        split_hi_loop(it, c + 2 * b, 4, slot)
                if attend and not last:
                    act.wait_ge(s_abs, a + 1)
                    act.activation(buf, buf, ACT.Exp, scale=-1.0).then_inc(s_ex, 1)
                if dense and l in (2, 4):
                    which = l // 2 - 1
                    act.wait_ge(s_read, P * 2 + (R_Q + which + 1))
                    if not (isinstance(P, int) and P < 2):
                        act.wait_ge(s_z, P * 6 - 6)
                    act.activation((qh, kh)[which][:, Pm, :], tmp[:, which, :], ACT.Copy,
                                   scale=(0.125, 1.0)[which]).then_inc(s_qh, 1)
                if attend and not last:
                    act.wait_ge(s_ex, a + 1)
                    act.activation(buf, buf, ACT.Ln, bias=1.0).then_inc(s_ln, 1)

            P_it = [None]

            def block_a(P, Pm, dense, attend):
                for l in range(6):
                    slot_a(P * 6 + (l - 6), (Pm * 6 + l - 6) % 12, P, Pm, l, dense, attend)

            def split_heads(L, p, done):
                act.wait_ge(s_unit, L * U_LAYER + U_O)
                act.wait_ge(s_og, done)
                act.activation(X(ph[0], p), tile(gp, p), ACT.Copy).then_inc(s_oh, 1)

            def out_project(L):
                v = 2 * L + 1

                def body(it):
                    for j in range(4):
                        k = it * 4 + j
                        if k >= 2:
                            split_hi(L * U_LAYER + U_O + k + 2, (k + 2) % 4, False)
                        if L == 0:
                            if k > 0:
                                act.wait_ge(s_brow, k)
                            act.activation(toh, oh, ACT.Copy, scale=tb[:, k:k + 1]).then_inc(s_toh, 1)
                        act.wait_ge(s_read, it * 4 + (L * R_LAYER + R_O + j + 1))
                        stream_hi(v, k, gcol(3 + L, k))
                        square(v, k, tile(h, k))
                        if k == 5:
                            embed(L)
                        if L == 0:
                            act.wait_ge(s_bst, 2 * k + 2)
                            act.dma_start(scratch[k], brow[k % 2]).then_inc(s_bout[k % 2], 16)
                for it in range(2):
                    body(it)

            def embed(L):
                act.wait_ge(s_p, 16 * (L + 1))
                act.activation(psplit[L][0][:, :, :], pstage[L][:, :, :], ACT.Copy).then_inc(s_pfh, 1)

            def embed_gate(L):
                for n in range(4):
                    u = L * U_LAYER + U_P + n
                    split_hi(u + 2, (u + 2) % 4, False)
                norm(2 * L + 1)
                act.preload_act_table(ACT.Sigmoid)
                v = 2 * L + 2
                for n in range(NT):
                    u = L * U_LAYER + U_T + n
                    if u + 2 < UNITS:
                        split_hi(u + 2, (u + 2) % 4, gained(u + 2))
                    act.wait_ge(s_read, L * R_LAYER + R_T + n + 1)
                    act.activation(tmp[:, n % 2, :], tmp[:, n % 2, :], ACT.Sigmoid).then_inc(s_sig, 1)
                    act.wait_ge(s_hg, 8 * L + n + 1)
                    if L == 0:
                        stream_hi(v, n, 1.0)
                    square(v, n, tile(h, n))

            def slot_b(a):
                if a % 4 == 0 and 0 <= a < NSB:
                    hd = a // 4 + 1
                    if 2 <= hd < HEADS_B:
                        act.wait_ge(s_ttr, 8 * (hd - 1))
                        load_bias(hd)
                if a >= 7 and (a - 7) % 4 == 0:
                    hd = (a - 7) // 4
                    act.wait_ge(s_pv, hd + 1)
                    if hd > 0:
                        act.wait_ge(s_nst, hd)
                    act.activation(sq[:, :], bank[7][:, :], ACT.Square).then_inc(s_osq, 1)
                if a >= 9 and a % 4 == 1:
                    hd = (a - 9) // 4
                    act.wait_ge(s_nst, hd + 1)
                    if hd > 0:
                        act.wait_ge(s_og, HEADS_A + 1 + hd)
                    act.activation(ssq[:, :], bank[6][:, :], ACT.Ln, scale=1.0 / 128, bias=EPS)\
                       .then_inc(s_nln, 1)
                    act.wait_ge(s_nln, hd + 1)
                    act.activation(ssq[:, :], ssq[:, :], ACT.Exp, scale=-0.5).then_inc(s_nrm, 1)
                if 0 <= a < NSB:
                    w = S - 128 * (a % 4)
                    act.wait_ge(s_nm, a + 1)
                    c = 8 * (a % 2)
                    act.activation(e1[:, a % 4, 0:w], e1[:, a % 4, 0:w], ACT.Exp, bias=small[:, c + 2:c + 3],
                                   accum_out=small[:, c + 4:c + 5]).then_inc(s_e, 1)
                    act.activation(e2[:, a % 2, 0:w], e2[:, a % 2, 0:w], ACT.Exp, bias=small[:, c + 3:c + 4],
                                   accum_out=small[:, c + 5:c + 6]).then_inc(s_e, 1)

            def copies_b(a):
                for n in range(3):
                    hd, r = divmod(a - 3 - n, 4)
                    if r == 0 and 0 <= hd < HEADS_B:
                        b, c, w = COPIES[n]
                        act.wait_ge(s_tr, 4 * hd + n + 2)
                        if hd > 0:
                            act.wait_ge(s_pv, hd)
                        act.activation(pth[:, c:c + w], bank[b][:, 0:w], ACT.Copy).then_inc(s_pth, 1)

            def load_bias(hd):
                src = scratch[hd].rearrange("p n -> (p n)")[127:127 + 128 * (BW - 1)]
                act.dma_start(bt[:, hd % 2, :], src.rearrange("(p n) -> p n", n=BW - 1)[:, 0:S])\
                   .then_inc(s_bt[hd % 2], 16)

            def weights_b(P, l):
                if P < 4 and l in Q_WEIGHTS:
                    u = U_LAYER + U_Q + 4 * P + Q_WEIGHTS.index(l) + 2
                    split_hi(u, u % 4, gained(u))

            def dense_b(P, l):
                if P < 4:
                    if l in Q_HI:
                        c = Q_HI.index(l)
                        act.wait_ge(s_read, R_LAYER + R_Q + 4 * P + c + 1)
                        if P >= 2:
                            act.wait_ge(s_s, 16 * (P - 1))
                        act.activation(bqk[c][0][:, P % 2, :], tmp[:, c % 2, :], ACT.Copy,
                                       scale=(1.0, 0.125)[c // 2]).then_inc(s_qh, 1)

            act.dma_start(tmp[:, 0, 0:256], lamp).then_inc(s_lp, 16)
            act.dma_start(sub[:, :], subln).then_inc(s_lp, 16)
            act.wait_ge(s_cst, 16)
            split_hi(0, 0, False)
            for k in range(NT):
                act.wait_ge(s_x[k // 2], 16)
                stream_hi(0, k, gcol(0, k))
                square(0, k, tile(h, k))
                if k == 1:
                    split_hi(1, 1, False)
            gate_project(0)
            values(0)
            act.preload_act_table_set("natural_log_exp_and_others")
            block_a(0, 0, True, False)
            block_a(1, 1, True, True)
            with act.Fori(1, 4) as it:
                P_it[0] = (it, 0)
                block_a(it * 2, 0, True, True)
                P_it[0] = (it, 1)
                block_a(it * 2 + 1, 1, True, True)
            for l in range(6):
                slot_a(42 + l, (42 + l) % 12, 8, 0, l, False, True)
                split_heads(0, l, 2 * l + 3)
                if l in (2, 4):
                    split_hi(U_O + 1 + l // 2, 1 + l // 2, False)
            act.wait_ge(s_ol, 2)
            act.dma_start(oh, onehot).then_inc(s_tb, 16)
            act.wait_ge(s_tb0, 1)
            act.dma_start(tb[0:NB, :], table).then_inc(s_tb, 16)
            for a in range(NGA, NGA + 2):
                slot_a(a, a % 12, 9, 1, 0, False, True)
            split_heads(0, 6, 15)
            split_heads(0, 7, 17)
            act.wait_ge(s_ol, NT)
            act.dma_start(pstage[0][:, :, :], pT[0].rearrange("k p t -> p k t")).then_inc(s_p, 16)
            act.wait_ge(s_tb, 32)
            out_project(0)
            embed_gate(0)
            gate_project(1)
            act.preload_act_table_set("natural_log_exp_and_others")
            for i in range(2):
                act.wait_ge(s_bout[i], 16 * (HEADS_B // 2))
            load_bias(0)
            load_bias(1)
            values(1)
            for P in range(5):
                for l in range(8):
                    dense_b(P, l)
                    slot_b(8 * P + l - 8)
                    weights_b(P, l)
                    dense_b(P, l + 0.5)
                    if P == 4 and l < 5:
                        split_heads(1, l, HEADS_A + l + 2)
                    if P == 4 and l in (5, 6):
                        split_hi(U_LAYER + U_O + l - 3, l - 3, False)
                    if P == 4 and l == 7:
                        split_heads(1, 5, HEADS_A + 7)
                    copies_b(8 * P + l - 8)
            for a in range(NSB, NSB + 6):
                slot_b(a)
                copies_b(a)
                if a == NSB + 3:
                    split_heads(1, 6, HEADS_A + 8)
            split_heads(1, 7, HEADS_A + 9)
            act.wait_ge(s_ol, 2 * NT)
            act.dma_start(pstage[1][:, :, :], pT[1].rearrange("k p t -> p k t")).then_inc(s_p, 16)
            out_project(1)
            embed_gate(1)
            norm(4)

        @block.vector
        def _(dve):
            def split_lo(u, slot):
                dve.wait_ge(s_wh, u + 1)
                dve.tensor_tensor(wl[:, slot, :], wf[:, slot % 2, :], wh[:, slot, :], ALU.subtract)\
                   .then_inc(s_wl, 1)

            def clear(v):
                if v > 0:
                    dve.wait_ge(s_stat, v)
                dve.memset(ssq[:, :], 0.0).then_inc(s_ss, 1)

            def stream_lo(v, k, gain):
                src, out, hi = tile(h, k), tile(pl[v % 2], k), tile(ph[v % 2], k)
                dve.wait_ge(s_xh, k + (8 * v + 1))
                if gain is None:
                    dve.tensor_tensor(out, src, hi, ALU.subtract).then_inc(s_xl, 1)
                else:
                    dve.scalar_tensor_tensor(out, src, gain, hi, ALU.mult, ALU.subtract).then_inc(s_xl, 1)

            def add_squares(v, k):
                dve.wait_ge(s_sq, k + (8 * v + 1))
                dve.wait_ge(s_ss, k + (9 * v + 1))
                dve.tensor_tensor(ssq[:, :], ssq[:, :], sq[:, :], ALU.add).then_inc(s_ss, 1)

            def scaled(u, r, slot, t):
                dve.wait_ge(s_unit, u + 1)
                dve.tensor_tensor(tmp[:, t, :], bank[slot % 2][:, :], rms[:, :], ALU.mult).then_inc(s_read, 1)

            def gate_project(L):
                for n in range(NT):
                    u, r = L * U_LAYER + U_G + n, L * R_LAYER + R_G + n
                    split_lo(u + 2, (u + 2) % 4)
                    if n == 0:
                        dve.wait_ge(s_rms, 4 * L + 2)
                    if n >= 2:
                        dve.wait_ge(s_silu, NT * L + n - 1)
                    scaled(u, r, n, n % 2)

            def values(L):
                dve.wait_ge(s_silu, NT * (L + 1))
                with dve.Fori(0, 2) as half:
                    for j in range(4):
                        c = L * U_LAYER + U_V + j + 2
                        split_lo(half * 4 + c, (j + 2) % 4)
                    for i in range(4):
                        dst = bass.ds(half * 512 + 1024 * i, 512)
                        dve.wait_ge(s_vh, half * 4 + (8 * L + i + 1))
                        dve.scalar_tensor_tensor(pl[1][:, dst], bank[2 + i][:, :], rmc[:, i:i + 1],
                                                 ph[1][:, dst], ALU.mult, ALU.subtract).then_inc(s_vl, 1)

            def slot_a(a, am, P, Pm, l, dense, attend):
                qh, ql, kh, kl = aqk
                if dense and l in (2, 4):
                    which = l // 2 - 1
                    scaled(P * 2 + (U_Q + which), None, which, which)
                if dense and l in (3, 5):
                    which = (l - 3) // 2
                    dst, hi = (ql, kl)[which], (qh, kh)[which]
                    dve.wait_ge(s_qh, P * 2 + (which + 1))
                    dve.scalar_tensor_tensor(dst[:, Pm, :], tmp[:, which, :], (0.125, 1.0)[which],
                                             hi[:, Pm, :], ALU.mult, ALU.subtract).then_inc(s_qk, 1)
                if attend and not (isinstance(a, int) and (a < 1 or a > NGA)):
                    b = (am - 1) % 12
                    w = GCOLS[b % 3]
                    dve.wait_ge(s_lh, a)
                    dve.tensor_tensor(all_[:, b % 4, 0:w], asp[:, b % 2, 0:w], alh[:, b % 4, 0:w],
                                      ALU.subtract).then_inc(s_ll, 1)
                if attend and not (isinstance(a, int) and (a < 2 or a > NGA + 1)):
                    b = (am - 2) % 12
                    w = GCOLS[b % 3]
                    dve.wait_ge(s_we, a - 1)
                    if not (isinstance(a, int) and a < 4):
                        dve.wait_ge(s_av, a - 3)
                    dve.tensor_copy(awh[:, b % 2, 0:w], aw[:, b % 2, 0:w]).then_inc(s_ph, 1)
                    dve.wait_ge(s_ph, a - 1)
                    dve.tensor_tensor(awl[:, b % 2, 0:w], aw[:, b % 2, 0:w], awh[:, b % 2, 0:w],
                                      ALU.subtract).then_inc(s_pl, 1)
                if attend and not (isinstance(a, int) and (a < 6 or a > NGA + 3)) and (am - 6) % 3 == 0:
                    hd = ((am - 6) // 3) % 2
                    head_out(a, hd, P, l)
                if dense and l in (0, 2):
                    split_lo(P * 2 + (U_Q + 2 + l // 2), (2 * Pm + 2 + l // 2) % 4)
                if attend and not (isinstance(a, int) and a >= NGA):
                    w = GCOLS[am % 3]
                    buf = asp[:, am % 2, 0:w]
                    dve.wait_ge(s_ln, a + 1)
                    dve.scalar_tensor_tensor(buf, bank[2 + am % 4][:, 0:w], 0.0, buf, ALU.max, ALU.add)\
                       .then_inc(s_sp, 1)

            def head_out(a, hd, P, l):
                p = P - 2
                rows = slice(64 * hd, 64 * hd + 64)
                t = gp[rows, p * S:(p + 1) * S] if isinstance(p, int) else gp[rows, bass.ds(p * S, S)]
                dve.wait_ge(s_av, a - 3)
                dve.tensor_tensor(t, bank[6 + hd][rows, :], t, ALU.mult).then_inc(s_og, 1)

            def block_a(P, Pm, dense, attend):
                for l in range(6):
                    slot_a(P * 6 + (l - 6), (Pm * 6 + l - 6) % 12, P, Pm, l, dense, attend)

            def split_heads(L, p):
                dve.wait_ge(s_oh, NT * L + p + 1)
                dve.tensor_tensor(X(pl[0], p), tile(gp, p), X(ph[0], p), ALU.subtract).then_inc(s_ol, 1)

            def out_project(L):
                v = 2 * L + 1

                def body(it):
                    for j in range(4):
                        c = L * U_LAYER + U_O + j
                        k = it * 4 + j
                        if k >= 2:
                            split_lo(it * 4 + (c + 2), (j + 2) % 4)
                        dve.wait_ge(s_unit, it * 4 + (c + 1))
                        dve.tensor_tensor(tile(h, k), tile(h, k), bank[j % 2][:, :], ALU.add).then_inc(s_read, 1)
                        stream_lo(v, k, gcol(3 + L, k))
                        add_squares(v, k)
                        if k == 6:
                            dve.wait_ge(s_pfh, L + 1)
                            dve.tensor_tensor(psplit[L][1][:, :, :], pstage[L][:, :, :], psplit[L][0][:, :, :],
                                              ALU.subtract).then_inc(s_pfl, 1)
                        if L == 0:
                            b = 2 + 2 * (k % 2)
                            dve.wait_ge(s_brow, k + 1)
                            if k >= 2:
                                dve.wait_ge(s_bout[k % 2], 16 * (k // 2))
                            dve.tensor_copy(brow[k % 2][:, 0:512], bank[b][:, :]).then_inc(s_bst, 1)
                            dve.tensor_copy(brow[k % 2][:, 512:BW], bank[b + 1][:, 0:BW - 512]).then_inc(s_bst, 1)
                for it in range(2):
                    body(it)

            def embed_gate(L):
                if L == 0:
                    for i in range(2):
                        dve.wait_ge(s_bout[i], 16 * (HEADS_B // 2))
                for n in range(4):
                    u = L * U_LAYER + U_P + n
                    split_lo(u + 2, (u + 2) % 4)
                    for nn in range(2):
                        dve.wait_ge(s_ple if nn == 0 else s_unit, 4 * L + n + 1 if nn == 0 else u + 1)
                        dve.tensor_copy(tile(gp, 2 * n + nn), bank[nn][:, :]).then_inc(s_read, 1)
                v = 2 * L + 2
                clear(v)
                dve.wait_ge(s_rms, 2 * (2 * L + 2))
                for n in range(NT):
                    u = L * U_LAYER + U_T + n
                    if u + 2 < UNITS:
                        split_lo(u + 2, (u + 2) % 4)
                    scaled(u, None, n, n % 2)
                    t = tmp[:, n % 2, :]
                    dve.wait_ge(s_sig, NT * L + n + 1)
                    dve.tensor_tensor(t, t, tile(gp, n), ALU.mult).then_inc(s_gm, 1)
                    dve.wait_ge(s_gm, NT * L + n + 1)
                    dve.tensor_tensor(tile(h, n), tile(h, n), t, ALU.add).then_inc(s_hg, 1)
                    if L == 0:
                        stream_lo(v, n, None)
                    add_squares(v, n)

            def combine(a):
                w, c = S - 128 * (a % 4), 8 * (a % 2)
                dve.wait_ge(s_e, 2 * a + 2)
                dve.reciprocal(small[:, c + 6:c + 8], small[:, c + 4:c + 6]).then_inc(s_rc, 1)
                dve.wait_ge(s_rc, a + 1)
                dve.tensor_scalar(small[:, c + 7:c + 8], small[:, c + 7:c + 8], lam[:, 3:4], None, ALU.mult)\
                   .then_inc(s_nr, 1)
                dve.tensor_scalar(e1[:, a % 4, 0:w], e1[:, a % 4, 0:w], small[:, c + 6:c + 7], None, ALU.mult)\
                   .then_inc(s_e1n, 1)
                dve.wait_ge(s_nr, a + 1)
                dve.wait_ge(s_e1n, a + 1)
                dve.scalar_tensor_tensor(e1[:, a % 4, 0:w], e2[:, a % 2, 0:w], small[:, c + 7:c + 8],
                                         e1[:, a % 4, 0:w], ALU.mult, ALU.add).then_inc(s_pr, 1)

            def slot_b(a):
                if a >= 10 and a % 4 == 2:
                    hd = (a - 10) // 4
                    dve.wait_ge(s_nrm, hd + 1)
                    dve.tensor_tensor(ssq[:, :], bank[7][:, :], ssq[:, :], ALU.mult).then_inc(s_on, 1)
                if 0 <= a < NSB:
                    hd = a // 4
                    w, c = S - 128 * (a % 4), 8 * (a % 2)
                    if a % 4 == 0:
                        dve.wait_ge(s_bt[hd % 2], 16 * (hd // 2) + 16)
                    if a >= 4:
                        dve.wait_ge(s_tr, a - 3)
                    if a >= 2:
                        dve.wait_ge(s_pr, a - 1)
                    for side, buf in enumerate((e1[:, a % 4, 0:w], e2[:, a % 2, 0:w])):
                        dve.wait_ge(s_s, 2 * a + side + 1)
                        dve.tensor_tensor_reduce(buf, bank[2 + side][:, 0:w], bt[:, hd % 2, S - w:S], 1.0, -3e38,
                                                 ALU.add, ALU.max, small[:, c + side:c + side + 1])\
                           .then_inc(s_ttr, 1)
                    dve.wait_ge(s_ttr, 2 * a + 2)
                    dve.tensor_scalar(small[:, c + 2:c + 4], small[:, c:c + 2], -1.0, None, ALU.mult)\
                       .then_inc(s_nm, 1)
                if 1 <= a < NSB + 1:
                    combine(a - 1)
                for n in range(3):
                    hd, r = divmod(a - 4 - n, 4)
                    if r == 0 and 0 <= hd < HEADS_B:
                        b, c, w = COPIES[n]
                        dve.wait_ge(s_pth, 3 * hd + n + 1)
                        dve.tensor_tensor(ptl[:, c:c + w], bank[b][:, 0:w], pth[:, c:c + w], ALU.subtract)\
                           .then_inc(s_pte, 1)

            def results_b(P, l):
                if P < 4:
                    if l in Q_READ:
                        c = Q_READ.index(l)
                        if 4 * P + c >= 2:
                            dve.wait_ge(s_qk, 2 * (HEADS_A // 2) + 4 * P + c - 1)
                        scaled(U_LAYER + U_Q + 4 * P + c, None, c, c % 2)
                    if l in Q_LO:
                        c = Q_LO.index(l)
                        dve.wait_ge(s_qh, 2 * (HEADS_A // 2) + 4 * P + c + 1)
                        dve.scalar_tensor_tensor(bqk[c][1][:, P % 2, :], tmp[:, c % 2, :], (1.0, 0.125)[c // 2],
                                                 bqk[c][0][:, P % 2, :], ALU.mult, ALU.subtract)\
                           .then_inc(s_qk, 1)

            def weights_b(P, l):
                if P < 4 and l in Q_WEIGHTS:
                    u = U_LAYER + U_Q + 4 * P + Q_WEIGHTS.index(l) + 2
                    split_lo(u, u % 4)

            dve.memset(tb[NB:NB + 1, :], NEG).then_inc(s_tb0, 1)
            dve.wait_ge(s_trf, 2)
            dve.tensor_scalar(neg1[:, :], ones[:, :], -1.0, None, ALU.mult).then_inc(s_one, 1)
            dve.tensor_copy(tri[:, :], trif[:, :]).then_inc(s_one, 1)
            dve.tensor_scalar(future[:, :], trif[:, :], -NEG, None, ALU.mult).then_inc(s_one, 1)
            dve.memset(small[:, 0:8], 0.0).then_inc(s_vl, 1)
            dve.memset(small[:, 8:16], 0.0).then_inc(s_og, 1)
            clear(0)
            dve.wait_ge(s_lp, 32)
            dve.tensor_tensor(lpp, lp[:, 0:4:2, :], lp[:, 1:4:2, :], ALU.mult).then_inc(s_lam, 1)
            dve.wait_ge(s_lam, 1)
            dve.tensor_reduce(lam[:, 0:2], lpp, AX.X, ALU.add).then_inc(s_lam, 1)
            dve.tensor_scalar(sub[:, :], sub[:, :], 1.0 - LAM_INIT, None, ALU.mult).then_inc(s_lam, 1)
            dve.wait_ge(s_cst, 16)
            split_lo(0, 0)
            dve.wait_ge(s_idn, 2)
            dve.tensor_copy(idr[:, :], trif[:, :]).then_inc(s_one, 1)
            for k in range(NT):
                stream_lo(0, k, gcol(0, k))
                add_squares(0, k)
                if k == 1:
                    split_lo(1, 1)
            gate_project(0)
            values(0)
            block_a(0, 0, True, False)
            block_a(1, 1, True, True)
            with dve.Fori(1, 4) as it:
                block_a(it * 2, 0, True, True)
                block_a(it * 2 + 1, 1, True, True)
            for l in range(6):
                slot_a(42 + l, (42 + l) % 12, 8, 0, l, False, True)
                split_heads(0, l)
                if l in (2, 4):
                    split_lo(U_O + 1 + l // 2, 1 + l // 2)
            for a in range(NGA, NGA + 4):
                slot_a(a, a % 12, 9, 1, a - NGA, False, True)
            split_heads(0, 6)
            split_heads(0, 7)
            clear(1)
            out_project(0)
            embed_gate(0)
            gate_project(1)
            dve.wait_ge(s_lame, 1)
            dve.tensor_tensor(lam[:, 2:3], lam[:, 1:2], lam[:, 0:1], ALU.subtract).then_inc(s_lam, 1)
            dve.wait_ge(s_lam, 4)
            dve.tensor_scalar(lam[:, 3:4], lam[:, 2:3], -LAM_INIT, None, ALU.add).then_inc(s_lam, 1)
            values(1)
            dve.wait_ge(s_lam, 5)
            for P in range(5):
                for l in range(8):
                    results_b(P, l)
                    slot_b(8 * P + l - 8)
                    weights_b(P, l)
                    results_b(P, l + 0.5)
                    if P == 4 and l < 5:
                        split_heads(1, l)
                    if P == 4 and l in (5, 6):
                        split_lo(U_LAYER + U_O + l - 3, l - 3)
                    if P == 4 and l == 7:
                        split_heads(1, 5)
            for a in range(NSB, NSB + 7):
                slot_b(a)
                if a == NSB + 3:
                    split_heads(1, 6)
            split_heads(1, 7)
            clear(3)
            out_project(1)
            embed_gate(1)
            dve.wait_ge(s_rms, 10)
            for k in range(NT):
                dve.scalar_tensor_tensor(tile(h, k), tile(h, k), gcol(5, k), rms[:, :], ALU.mult, ALU.mult)\
                   .then_inc(s_fin, 1)

        @block.gpsimd
        def _(pool):
            pool.memset(ones[:, :], 1.0).then_inc(s_trf, 1)
            pool.memset(trif[:, :], -1.0).then_inc(s_t0, 1)
            pool.wait_ge(s_t0, 1)
            pool.affine_select(out=trif[:, :], in_=trif[:, :], compare_op=ALU.is_ge, fill=0.0, base=0,
                               pattern=[[-1, 128]], channel_multiplier=1).then_inc(s_trf, 1)
            pool.wait_ge(s_one, 3)
            pool.memset(trif[:, :], 0.0).then_inc(s_idn, 1)
            pool.wait_ge(s_idn, 1)
            pool.affine_select(out=trif[:, :], in_=trif[:, :], compare_op=ALU.not_equal, fill=1.0, base=0,
                               pattern=[[-1, 128]], channel_multiplier=1).then_inc(s_idn, 1)

            def value_columns(n, slot):
                for src, dst in ((ph[1], vph), (pl[1], vpl)):
                    view = src[:, :].rearrange("p (i c) -> p i c", i=4)
                    pool.tensor_copy(dst[:, slot, :, :], view[:, :, bass.ds(n * 128, 128)]).then_inc(s_vp, 1)

            def pair_columns(P, Pm):
                if not (isinstance(P, int) and P < 2):
                    pool.wait_ge(s_av, P * 6 - 6)
                value_columns(P, Pm)

            pool.wait_ge(s_vl, 9)
            pair_columns(0, 0)
            pair_columns(1, 1)
            with pool.Fori(1, 4) as it:
                pair_columns(it * 2, 0)
                pair_columns(it * 2 + 1, 1)

            def gain(u, g, per):
                k0 = 0 if per == 128 else 2 * (u % 4)
                t = wf[:, u % 2, :].rearrange("p (k c) -> p k c", c=per)
                n = UNIT // per
                pool.wait_ge(s_wd[u % 2], 16 * (u // 2) + 16)
                col = gn[:, g * NT + k0:g * NT + k0 + n].rearrange("p (k o) -> p k o", o=1).to_broadcast([128, n, per])
                pool.tensor_tensor(t, t, col, ALU.mult).then_inc(s_wg, 1)

            def gate_head(a):
                hd = (a - 10) // 4
                pool.wait_ge(s_on, hd + 1)
                pool.tensor_tensor(tile(gp, hd), ssq[:, :], tile(gp, hd), ALU.mult).then_inc(s_og, 1)

            for n in range(U_V):
                gain(U_LAYER + U_G + n, 2, 128)
            for n in range(U_Q - U_V):
                gain(U_LAYER + U_V + n, 1, 512)
                if n < 4:
                    for m in range(2 * n, 2 * n + 2):
                        pool.wait_ge(s_silu, NT + m + 1)
                        if m == 0:
                            pool.wait_ge(s_lam, 3)
                        pool.tensor_scalar(tile(gp, m), tile(gp, m), sub[:, 0:1], None, ALU.mult).then_inc(s_silc, 1)
            q_units = [(U_LAYER + U_Q + n, 1 if n % 4 < 2 else 2) for n in range(16)]
            for n in range(2):
                gain(*q_units.pop(0), 128)
            pool.wait_ge(s_vl, 17)
            for P in range(5):
                for l in range(8):
                    a = 8 * P + l - 8
                    if P < 4 and l in Q_WEIGHTS and q_units:
                        gain(*q_units.pop(0), 128)
                    if a >= 10 and a % 4 == 2:
                        gate_head(a)
            for a in range(NSB, NSB + 7):
                if a % 4 == 2:
                    gate_head(a)


def bucket_rows():
    dist = 511 - np.arange(BW)
    n = np.maximum(dist, 0)
    nf = np.maximum(n, 1).astype(np.float32)
    half = NB // 2
    large = half + (np.log(nf / half) / np.float32(math.log(128 / half)) * (NB - half)).astype(np.int32)
    b = np.where(n < half, n, np.minimum(large, NB - 1))
    rows = np.zeros((NB + 1, BW), np.float32)
    for j in range(BW):
        rows[b[j] if dist[j] >= 0 else NB, j] = 1.0
    return rows


def kernel(x, p, attn_norm, w_in_a, w_out_a, kv_norm, w_kv, w_q_b, diff_lambda, diff_subln, w_out_b,
           rel_bias, ple_norm, w_ple_proj, w_ple_gate, final_norm):
    import concourse.bacc as _bacc
    from concourse.bass_utils import run_bass_kernel_spmd as _run

    def cols(w):
        k, n = w.shape
        return w.reshape(k // 128, 128, n // 128, 128).transpose(2, 1, 0, 3).reshape(n // 128, 128, -1)

    def slabs(w):
        return w.reshape(4, 2, 128, w.shape[1] // 512, 512).transpose(3, 0, 2, 1, 4).reshape(-1, 128, UNIT)

    def pairs(w):
        u = cols(w).reshape(4, 2, 128, 256).transpose(0, 2, 1, 3).reshape(4, 128, 512)
        return np.concatenate([u, np.zeros_like(u)], axis=2)

    def woven(*parts):
        return np.stack(parts, axis=1).reshape(-1, 128, UNIT)

    w_in, w_oa, w_qb, w_ob = w_in_a[0], w_out_a[0], w_q_b[0], w_out_b[0]
    units = np.concatenate([
        cols(w_in[:, 3 * D:]), slabs(w_in[:, 2 * D:3 * D]),
        woven(cols(w_in[:, :D]), cols(w_in[:, D:2 * D])),
        cols(w_oa), pairs(w_ple_proj[0]), cols(w_ple_gate[0]),
        cols(w_qb[:, D:]), slabs(w_kv[:, D:]),
        woven(cols(w_kv[:, :512]), cols(w_kv[:, 512:D]), cols(w_qb[:, :512]), cols(w_qb[:, 512:D])),
        cols(w_ob), pairs(w_ple_proj[1]), cols(w_ple_gate[1])])
    gains = np.stack([attn_norm[0], kv_norm, attn_norm[1], ple_norm[0], ple_norm[1], final_norm])
    arrays = {
        "xT": x[0].T.reshape(NT, 128, S),
        "pT": p[:, 0].transpose(0, 2, 1).reshape(2, DP // 128, 128, S),
        "w_units": units,
        "gains": gains.reshape(6, NT, 128).transpose(2, 0, 1).reshape(128, 6 * NT),
        "subln": diff_subln.reshape(128, 1),
        "lamp": np.broadcast_to(diff_lambda.reshape(1, 256), (128, 256)),
        "table": rel_bias,
        "onehot": bucket_rows(),
    }
    arrays = {f"in_{n}": np.ascontiguousarray(v) for n, v in arrays.items()}
    nc = _bacc.Bacc("TRN2", target_bir_lowering=False, num_devices=1)
    ins = [nc.dram_tensor(n, v.shape, F32, kind="ExternalInput").ap() for n, v in arrays.items()]
    scratch = nc.dram_tensor("bias_rows", (HEADS_B, 128, BW), F32, kind="Internal").ap()
    outT = nc.dram_tensor("outT", (NT, 128, S), F32, kind="ExternalOutput").ap()
    build(nc, *ins, scratch, outT)
    got = _run(nc, [arrays], core_ids=[0]).results[0]["outT"]
    return np.ascontiguousarray(got.reshape(D, S).T).reshape(1, S, D)
```

```python
from contextlib import ExitStack
import math

import numpy as np
import concourse.bass as bass
from concourse import mybir

F32 = mybir.dt.float32
F32R = mybir.dt.float32r
ALU = mybir.AluOpType
ACT = mybir.ActivationFunctionType
AX = mybir.AxisListType

D = 1024
S = 512
NT = D // 128
DP = 256
HEADS_A = 16
HEADS_B = 8
NB = 32
EPS = 1e-6
LAM_INIT = 0.8 - 0.6 * math.exp(-0.3 * 1)
NEG = -1e30
UNIT = 1024

U_G, U_V, U_Q, U_O, U_P, U_T, U_LAYER = 0, 8, 16, 32, 40, 44, 52
R_G, R_Q, R_O, R_P, R_T, R_LAYER = 0, 8, 24, 32, 40, 48
UNITS = 2 * U_LAYER

BW = 640
GROUPS = [[(3, 0), (2, 128)], [(1, 0)], [(0, 0)]]
GCOLS = [384, 384, 512]
TAILS = [slice(128, 384), slice(0, 384)]
NGA = 3 * HEADS_A
LAST = NGA - 6
NSB = 4 * HEADS_B
Q_TILES = [0, 5, 10, 16, 21, 26, 30, 32, 32]
Q_READ, Q_HI, Q_LO, Q_WEIGHTS = (2, 3, 5, 6.25), (2.5, 3.5, 5.5, 6.5), (3, 4, 6, 7), (0, 1, 4, 7)
G_BANKS = [2, 3, 4, 5]
V_BANKS = [[6, 7, 0, 1], [2, 3, 6, 7]]
O_BANKS = [0, 1, 2, 3]
P_BANKS = [6, 7, 0, 1]
COPIES = [(6, 1024, 256), (5, 512, 512), (4, 0, 512)]
FINAL = [[0, 2, 3, 5, 7], [1, 4, 6]]
NORMED = [2, 3, 5, 6, 7]


def tails(P, m):
    return P * 4 + (2 * (m // 3) + min(m % 3 + 1, 2) - 4)


def build(nc, xT, pT, w_units, gains, subln, lamp, table, onehot, scratch, outT):
    with ExitStack() as ctx:
        def sb(name, shape, dt=F32, where=ctx):
            return where.enter_context(nc.sbuf_tensor(name, shape, dt))

        def sem(name):
            return ctx.enter_context(nc.semaphore(name))

        bank = [ctx.enter_context(nc.psum_tensor(f"bank{i}", [128, 512], F32)) for i in range(8)]

        h = sb("h", [128, NT * S])
        ph = [sb(f"split{i}_hi", [128, NT * S], F32R) for i in range(2)]
        pl = [sb(f"split{i}_lo", [128, NT * S], F32R) for i in range(2)]
        gp = sb("gp", [128, NT * S])
        wf = sb("w_f32", [128, 2, UNIT])
        wh = sb("w_hi", [128, 4, UNIT], F32R)
        wl = sb("w_lo", [128, 4, UNIT], F32R)
        rms = sb("rms", [128, S])
        rmc = sb("rms_col", [128, 4])
        ssq = sb("ssq", [128, S])
        sq = sb("sq", [128, S])
        tmp = sb("tmp", [128, 2, S])
        ones = sb("ones", [128, 128])
        trif = sb("trif", [128, 128])
        gn = sb("gains_sb", [128, 6 * NT])
        sub = sb("subln_sb", [128, 1])
        lp = tmp[:, 0, 0:256].rearrange("p (a d) -> p a d", a=4)
        lpp = tmp[:, 1, 0:128].rearrange("p (a d) -> p a d", a=2)
        lam = sb("lam", [128, 4])
        tb = sb("table_sb", [NB + 1, HEADS_B])
        small = sb("small", [128, 16])

        tA, tB = ExitStack(), ExitStack()
        with tA:
            vph = sb("v_cols_hi", [128, 2, 4, 128], F32R, tA)
            vpl = sb("v_cols_lo", [128, 2, 4, 128], F32R, tA)
            neg1 = sb("neg1", [128, 128], F32R, tA)
            future = sb("future", [128, 2, 128], F32R, tA)
            idr = sb("identity_r", [128, 128], F32R, tA)
            tri = sb("tri", [128, 128], F32R, tA)
            asp = sb("sp", [128, 3, S], F32, tA)
            aw = sb("w_att", [128, 2, S], F32, tA)
            alh = sb("l_hi", [128, 2, S], F32R, tA)
            all_ = sb("l_lo", [128, 2, S], F32R, tA)
            tsh = sb("tail_hi", [128, 2, 384], F32R, tA)
            tsl = sb("tail_lo", [128, 2, 384], F32R, tA)
            awh = sb("wa_hi", [128, 2, S], F32R, tA)
            awl = sb("wa_lo", [128, 2, S], F32R, tA)
            aqk = [sb(n, [128, 2, S], F32R, tA) for n in ("a_qh", "a_ql", "a_kh", "a_kl")]
        with tB:
            e1 = sb("e1", [128, 4, S], F32, tB)
            e2 = sb("e2", [128, 2, S], F32, tB)
            bt = sb("bias_tile", [128, 2, S], F32, tB)
            pth = sb("pt_hi", [128, 1280], F32R, tB)
            ptl = sb("pt_lo", [128, 1280], F32R, tB)
            bqk = [[sb(f"b_{n}{q}", [128, 2, S], F32R, tB) for q in "hl"] for n in ("k1", "k2", "q1", "q2")]
        pstage = [asp[:, 0:2, :], e2[:, :, :]]
        psplit = [(aqk[0], aqk[1]), (bqk[0][0], bqk[0][1])]
        e1_flat, e2_flat = e1[:, :, :].rearrange("p a n -> p (a n)"), e2[:, :, :].rearrange("p a n -> p (a n)")
        oh = e1_flat[0:NB + 1, 0:BW]
        toh = e1_flat[0:NB + 1, BW:2 * BW]
        brow = [e1_flat[:, 2 * BW:3 * BW], e2_flat[:, 0:BW]]

        s_x = [sem(f"s_x{i}") for i in range(4)]
        s_cst = sem("s_cst")
        s_lp = sem("s_lp")
        s_tb = sem("s_tb")
        s_p = sem("s_p")
        s_wd = [sem(f"s_wd{i}") for i in range(2)]
        s_trf = sem("s_trf")
        s_t0 = sem("s_t0")
        s_one = sem("s_one")
        s_idn = sem("s_idn")
        s_tb0 = sem("s_tb0")
        s_lam = sem("s_lam")
        s_lame = sem("s_lame")
        s_wg = sem("s_wg")
        s_wh = sem("s_wh")
        s_wl = sem("s_wl")
        s_unit = sem("s_unit")
        s_ple = sem("s_ple")
        s_read = sem("s_read")
        s_vres = sem("s_vres")
        s_vh = sem("s_vh")
        s_vl = sem("s_vl")
        s_silu = sem("s_silu")
        s_silc = sem("s_silc")
        s_qh = sem("s_qh")
        s_qk = sem("s_qk")
        s_xh = sem("s_xh")
        s_xl = sem("s_xl")
        s_sq = sem("s_sq")
        s_ss = sem("s_ss")
        s_stat = sem("s_stat")
        s_lnr = sem("s_lnr")
        s_rms = sem("s_rms")
        s_z = sem("s_z")
        s_abs = sem("s_abs")
        s_ex = sem("s_ex")
        s_ln = sem("s_ln")
        s_sp = sem("s_sp")
        s_lh = sem("s_lh")
        s_ll = sem("s_ll")
        s_ts = sem("s_ts")
        s_th = sem("s_th")
        s_tl = sem("s_tl")
        s_tri = sem("s_tri")
        s_we = sem("s_we")
        s_ph = sem("s_ph")
        s_pl = sem("s_pl")
        s_vp = sem("s_vp")
        s_av = sem("s_av")
        s_og = sem("s_og")
        s_oh = sem("s_oh")
        s_ol = sem("s_ol")
        s_toh = sem("s_toh")
        s_brow = sem("s_brow")
        s_bst = sem("s_bst")
        s_bout = [sem(f"s_bout{i}") for i in range(2)]
        s_bt = [sem(f"s_bt{i}") for i in range(2)]
        s_pfh = sem("s_pfh")
        s_pfl = sem("s_pfl")
        s_sig = sem("s_sig")
        s_gm = sem("s_gm")
        s_hg = sem("s_hg")
        s_s = sem("s_s")
        s_ttr = sem("s_ttr")
        s_nm = sem("s_nm")
        s_e = sem("s_e")
        s_rc = sem("s_rc")
        s_nr = sem("s_nr")
        s_e1n = sem("s_e1n")
        s_pr = sem("s_pr")
        s_tr = sem("s_tr")
        s_pth = sem("s_pth")
        s_pte = sem("s_pte")
        s_pv = sem("s_pv")
        s_osq = sem("s_osq")
        s_nst = sem("s_nst")
        s_nln = sem("s_nln")
        s_nrm = sem("s_nrm")
        s_on = sem("s_on")
        s_hgain = sem("s_hgain")
        s_fin = [sem(f"s_fin{i}") for i in range(2)]
        s_out = sem("s_out")

        def X(which, k, part=slice(0, S)):
            return which[:, k * S + part.start:k * S + part.stop]

        def tile(buf, k):
            return buf[:, k * S:(k + 1) * S] if isinstance(k, int) else buf[:, bass.ds(k * S, S)]

        def gcol(g, k):
            return gn[:, g * NT + k:g * NT + k + 1] if isinstance(k, int) else gn[:, bass.ds(k + g * NT, 1)]

        def gained(u):
            return U_LAYER <= u < U_LAYER + U_O

        block = ctx.enter_context(nc.Block())

        @block.sync
        def _(sp):
            sp.dma_start(gn[:, :], gains).then_inc(s_cst, 16)
            sp.dma_start(wf[:, 0, :], w_units[0]).then_inc(s_wd[0], 16)
            for i in range(4):
                sp.dma_start(h[:, 2 * i * S:(2 * i + 2) * S].rearrange("p (k t) -> p k t", k=2),
                             xT[2 * i:2 * i + 2].rearrange("k p t -> p k t")).then_inc(s_x[i], 16)
                if i == 0:
                    sp.dma_start(wf[:, 1, :], w_units[1]).then_inc(s_wd[1], 16)
            with sp.Fori(1, UNITS // 2) as i:
                for slot in range(2):
                    sp.wait_ge(s_wl, i * 2 + (slot - 1))
                    sp.dma_start(wf[:, slot:slot + 1, :],
                                 w_units.rearrange("u p n -> p u n")[:, bass.ds(i * 2 + slot, 1), :])\
                      .then_inc(s_wd[slot], 16)
            for k in range(NT):
                by = 0 if k in FINAL[0] else 1
                sp.wait_ge(s_fin[by], FINAL[by].index(k) + 1)
                sp.dma_start(outT[k], tile(h, k)).then_inc(s_out, 16)
            sp.wait_ge(s_out, 16 * NT)
            for i in range(2):
                sp.wait_ge(s_bout[i], 16 * (HEADS_B // 2))

        @block.tensor
        def _(pe):
            def mm3(out, lh, ll, rh, rl, start, stop):
                pe.matmul(out, lhsT=lh, rhs=rh, start=start, stop=False, skip_group_check=True)
                pe.matmul(out, lhsT=lh, rhs=rl, start=False, stop=False, skip_group_check=True)
                return pe.matmul(out, lhsT=ll, rhs=rh, start=False, stop=stop, skip_group_check=True)

            def product(slot, which, k, start, stop, b):
                c = slice(128 * k, 128 * k + 128)
                return mm3(bank[b][:, :], wh[:, slot, c], wl[:, slot, c],
                           X(ph[which], k), X(pl[which], k), start, stop)

            def open_unit(u, r):
                pe.wait_ge(s_wl, u + 1)
                pe.wait_ge(s_read, r - 1)

            def stat(v):
                pe.wait_ge(s_ss, 9 * (v + 1))
                last = pe.matmul(bank[6][:, :], lhsT=ones[:, :], rhs=ssq[:, :], start=True, stop=True)
                for i in (range(4) if v in (0, 2) else ()):
                    last = pe.matmul(bank[7][:, i:i + 1], lhsT=ssq[:, 128 * i:128 * i + 128],
                                     rhs=ones[:, 0:1], start=(i == 0), stop=True, skip_group_check=True)
                last.then_inc(s_stat, 1)

            def bias_row(hd):
                pe.wait_ge(s_toh, hd + 1)
                if hd == 0:
                    pe.wait_ge(s_read, R_LAYER + R_G + NT)
                else:
                    pe.wait_ge(s_bst, 2 * hd)
                pe.matmul(bank[4][:, :], lhsT=ones[0:NB + 1, :], rhs=toh[:, 0:512], start=True, stop=True)
                pe.matmul(bank[5][:, 0:BW - 512], lhsT=ones[0:NB + 1, :], rhs=toh[:, 512:BW],
                          start=True, stop=True).then_inc(s_brow, 1)

            def values(L):
                for half in range(2):
                    if half == 1:
                        pe.wait_ge(s_read, L * R_LAYER + R_G + NT)
                    for j in range(4):
                        u = L * U_LAYER + U_V + 4 * half + j
                        pe.wait_ge(s_wl, u + 1)
                        for i in range(4):
                            if half == 1 and j == 0 and i >= 2:
                                pe.wait_ge(s_vl, 8 * L + i - 1)
                            rows = slice(128 * i, 128 * i + 128)
                            for kk in range(2):
                                k = 2 * j + kk
                                c = slice(512 * kk, 512 * kk + 512)
                                last = mm3(bank[V_BANKS[half][i]][:, :], X(ph[0], k, rows), X(pl[0], k, rows),
                                           wh[:, j, c], wl[:, j, c], k == 0, k == NT - 1)
                            if j == 3 and i < 3:
                                last.then_inc(s_vres, 1)
                        last.then_inc(s_unit, 1)
                        if L == 1:
                            bias_row(4 * half + j)
                pe.wait_ge(s_vl, 8 * L + 4)

            def scores_a(a, am, P):
                g, hd = am % 3, (am // 3) % 2
                z = bank[2 + am % 4]
                par = (am // 6) % 2
                if am % 6 == 0:
                    pe.wait_ge(s_qk, P * 2)
                if not isinstance(a, int) or a >= 4:
                    pe.wait_ge(s_we, a - 3)
                qh, ql, kh, kl = aqk
                rows = slice(64 * hd, 64 * hd + 64)
                for n, (i, off) in enumerate(GROUPS[g]):
                    w = S - 128 * i
                    o = z[:, off:off + w]
                    kc, qc = slice(128 * i, 128 * i + 128), slice(128 * i, S)
                    last = mm3(o, kh[rows, par, kc], kl[rows, par, kc], qh[rows, par, qc], ql[rows, par, qc],
                               n == 0, True)
                n = len(GROUPS[g])
                last = pe.matmul(z[:, 0:128 * n], lhsT=idr[:, :], rhs=future[:, 0:n, :], start=False, stop=True,
                                 skip_group_check=True)
                last.then_inc(s_z, 1)

            def logsums(a, am, P, m):
                g = am % 3
                z = bank[2 + am % 4]
                pe.wait_ge(s_ll, a + 1)
                if g > 0:
                    pe.wait_ge(s_tl, tails(P, m - 1))
                terms = [(tri, off, part[:, am % 2, off:off + S - 128 * i])
                         for i, off in GROUPS[g] for part in (alh, all_)]
                if g == 0:
                    terms += [(neg1, 256, part[:, am % 2, 0:128]) for part in (alh, all_)]
                else:
                    w = TAILS[g - 1].stop - TAILS[g - 1].start
                    terms += [(neg1, 128, part[:, g - 1, 0:w]) for part in (tsh, tsl)]
                for st, off, logs in terms:
                    last = pe.matmul(z[:, off:off + logs.shape[-1]], lhsT=st[:, :], rhs=logs, start=False,
                                     stop=True, skip_group_check=True)
                last.then_inc(s_tri, 1)

            def heads_a(a, am, P):
                g, hd = am % 3, (am // 3) % 2
                par = (am // 6) % 2
                o = bank[6 + hd]
                pe.wait_ge(s_pl, a + 1)
                if g == 0:
                    if hd == 0:
                        pe.wait_ge(s_vp, P * 2)
                    pe.wait_ge(s_og, P * 2 + (hd - 2))
                for i, off in GROUPS[g]:
                    w = S - 128 * i
                    last = mm3(o[:, 128 * i:S], vph[:, par, i, :], vpl[:, par, i, :],
                               awh[:, am % 2, off:off + w], awl[:, am % 2, off:off + w], i == 3, True)
                last.then_inc(s_av, 1)

            def block_a(P, Pm, dense, attend):
                u0 = P * 2 + U_Q
                for l in range(6):
                    am = (Pm * 6 + l - 6) % 12
                    a = P * 6 + (l - 6)
                    first = isinstance(a, int) and a == 0
                    if attend and not first:
                        scores_a(a, am, P)
                    if attend and not (isinstance(a, int) and a < 2):
                        logsums(a - 2, (am - 2) % 12, P, l - 2)
                    if dense and l < 4:
                        c = l // 2
                        slot = (2 * Pm + c) % 4
                        if l % 2 == 0:
                            open_unit(u0 + c, P * 2 + (R_Q + c))
                        for k in range(4 * (l % 2), 4 * (l % 2) + 4):
                            last = product(slot, 0, k, k == 0, k == NT - 1, c)
                        if l % 2:
                            last.then_inc(s_unit, 1)
                    if attend and first:
                        scores_a(a, am, P)
                    if not dense and l > 0:
                        out_early(0, l - 1, (0, 1))
                    if attend and not (isinstance(a, int) and a < 3):
                        heads_a(a - 3, (am - 3) % 12, P if l >= 3 else P - 1)

            def gate_tiles(L):
                with pe.Fori(0, 2) as it:
                    for j in range(4):
                        open_unit(it * 4 + (L * U_LAYER + U_T + j), it * 4 + (L * R_LAYER + R_T + j))
                        for k in range(NT):
                            if j == 0:
                                pe.wait_ge(s_xl, 8 * (2 * L + 1) + k + 1)
                            last = product(j, 1, k, k == 0, k == NT - 1, j % 2)
                        last.then_inc(s_unit, 1)

            def out_early(L, k, units):
                for c in units:
                    if k == 0:
                        pe.wait_ge(s_wl, L * U_LAYER + U_O + c + 1)
                        if c < 2:
                            pe.wait_ge(s_read, L * R_LAYER + R_O + c - 1)
                        elif L == 0:
                            pe.wait_ge(s_we, NGA - 2)
                        else:
                            pe.wait_ge(s_ttr, 2 * NSB)
                    pe.wait_ge(s_ol, NT * L + k + 1)
                    product(c, 0, k, k == 0, False, O_BANKS[c])

            def scores_b(a, P):
                i = 3 - a % 4
                hd = a // 4
                if a % 8 == 0:
                    pe.wait_ge(s_qk, HEADS_A + 4 * P)
                rows = slice(64 * (hd % 2), 64 * (hd % 2) + 64)
                par = (P - 1) % 2
                w = 128 * i + 128
                qc = slice(128 * i, 128 * i + 128)
                for side in range(2):
                    kh, kl = bqk[side]
                    qh, ql = bqk[2 + side]
                    if a >= 1:
                        pe.wait_ge(s_ttr, 2 * a - 1 + side)
                    mm3(bank[2 + side][:, 0:w], qh[rows, par, qc], ql[rows, par, qc],
                        kh[rows, par, 0:w], kl[rows, par, 0:w], True, True).then_inc(s_s, 1)

            PT = [(4, 0, 0, 2), (5, 0, 512, 1), (6, 0, 1024, 0), (5, 384, 896, 1)]

            def transposes(a, late=False):
                hd, i = a // 4, 3 - a % 4
                if not late:
                    pe.wait_ge(s_pr, a + 1)
                for j in (0,) if late else (2, 3, 1) if i == 3 else (2, 1, 0)[2 - i:]:
                    b, c, _, copy = PT[j]
                    if i == 3 and hd > 0:
                        pe.wait_ge(s_pte, 3 * hd - 2 + copy)
                    if i == 3 and j == 2 and hd > 1:
                        pe.wait_ge(s_nln, hd - 1)
                    c += 128 * (i - j)
                    last = pe.transpose(bank[b][:, c:c + 128], e1[:, a % 4, 128 * j:128 * j + 128], trif[:, :])
                if late or i < 3:
                    last.then_inc(s_tr, 1)

            def head_b(hd):
                if hd > 0:
                    pe.wait_ge(s_on, hd)
                for j in (2, 3, 1, 0):
                    w = S - 128 * j
                    _, _, c, copy = PT[j]
                    pe.wait_ge(s_pte, 3 * hd + 1 + copy)
                    v = slice(UNIT * j + 128 * hd, UNIT * j + 128 * hd + 128)
                    last = mm3(bank[7][:, 128 * j:S], ph[1][:, v], pl[1][:, v],
                               pth[:, c:c + w], ptl[:, c:c + w], j == 2, True)
                last.then_inc(s_pv, 1)

            def head_stat(hd):
                pe.wait_ge(s_osq, hd + 1)
                if hd < HEADS_B - 1:
                    pe.wait_ge(s_pte, 3 * hd + 4)
                pe.matmul(bank[6][:, :], lhsT=ones[:, :], rhs=sq[:, :], start=True, stop=True).then_inc(s_nst, 1)

            def block_b(P):
                for l in range(8):
                    a = 8 * P + l - 8
                    if 0 < a < NSB:
                        scores_b(a, P)
                    if a >= 3 and a % 4 == 3:
                        transposes(a - 3, late=True)
                    if a >= 7 and a % 4 == 3:
                        head_b(a // 4 - 1)
                    if P == 4 and 1 <= l < 6:
                        out_early(1, l - 1, (0, 1))
                    if P < 4:
                        for m in range(Q_TILES[l], Q_TILES[l + 1]):
                            c, k = m // 8, m % 8
                            if k == 0:
                                open_unit(U_LAYER + U_Q + 4 * P + c, R_LAYER + R_Q + 4 * P + c)
                            last = product(c, 0, k, k == 0, k == NT - 1, c % 2)
                            if k == NT - 1:
                                last.then_inc(s_unit, 1)
                    if a == 0:
                        scores_b(a, P)
                    tail_b(a)

            def tail_b(a):
                if 2 <= a < NSB + 2:
                    transposes(a - 2)
                if a >= 8 and a % 4 == 0:
                    head_stat((a - 8) // 4)

            def gate_project(L):
                v = 2 * L
                for k, c in [(0, 0), (1, 0), (0, 1), (1, 1)] + [(k, c) for k in range(2, NT) for c in range(2)]:
                    if k == 0:
                        pe.wait_ge(s_wl, L * U_LAYER + U_G + c + 1)
                    pe.wait_ge(s_xl, 8 * v + k + 1)
                    last = product(c, 0, k, k == 0, k == NT - 1, G_BANKS[c])
                    if k == NT - 1:
                        last.then_inc(s_unit, 1)
                for n in range(2, NT):
                    if n == (4, 2)[L]:
                        stat(v)
                    pe.wait_ge(s_wl, L * U_LAYER + U_G + n + 1)
                    if n >= 4:
                        pe.wait_ge(s_read, L * R_LAYER + R_G + n - 3)
                    for k in range(NT):
                        last = product(n % 4, 0, k, k == 0, k == NT - 1, G_BANKS[n % 4])
                    last.then_inc(s_unit, 1)

            def rest(L):
                base = L * U_LAYER
                for k, n in ((6, 0), (6, 1), (6, 2), (7, 0), (6, 3), (7, 1), (7, 2), (7, 3)):
                    pe.wait_ge(s_ol, NT * L + k + 1)
                    last = product(n, 0, k, False, k == NT - 1, O_BANKS[n])
                    if k == NT - 1:
                        last.then_inc(s_unit, 1)
                for n in range(4, NT):
                    pe.wait_ge(s_wl, base + U_O + n + 1)
                    pe.wait_ge(s_read, L * R_LAYER + R_O + n - 3)
                    for k in range(NT):
                        last = product(n % 4, 0, k, k == 0, k == NT - 1, O_BANKS[n % 4])
                    last.then_inc(s_unit, 1)
                pe.wait_ge(s_pfl, L + 1)
                fh, fl = psplit[L]
                for n in range(4):
                    pe.wait_ge(s_wl, base + U_P + n + 1)
                    for nn in range(2):
                        r = 2 * n + nn
                        if r >= 2:
                            pe.wait_ge(s_read, L * R_LAYER + R_P + r - (5 if r < 4 else 3))
                        for kk in range(2):
                            c = slice(128 * (2 * nn + kk), 128 * (2 * nn + kk) + 128)
                            last = mm3(bank[P_BANKS[r % 4]][:, :], wh[:, n, c], wl[:, n, c], fh[:, kk, :],
                                       fl[:, kk, :], kk == 0, kk == 1)
                        last.then_inc(s_ple if nn == 0 else s_unit, 1)
                pe.wait_ge(s_read, L * R_LAYER + R_P + 6)
                stat(2 * L + 1)
                gate_tiles(L)

            gate_project(0)
            values(0)
            pe.wait_ge(s_one, 5)
            block_a(0, 0, True, False)
            block_a(1, 1, True, True)
            with pe.Fori(1, 4) as it:
                block_a(it * 2, 0, True, True)
                block_a(it * 2 + 1, 1, True, True)
            block_a(8, 0, False, True)
            for a in range(NGA, NGA + 3):
                for k in range(2 * (a - NGA), 2 * (a - NGA) + 2):
                    out_early(0, k, (2, 3))
                if a == NGA + 1:
                    out_early(0, 5, (0, 1))
                if a < NGA + 2:
                    logsums(a - 2, (a - 2) % 12, 8, a - 2 - LAST)
                heads_a(a - 3, (a - 3) % 12, 8)
            rest(0)
            gate_project(1)
            values(1)
            pe.wait_ge(s_idn, 2)
            for P in range(5):
                block_b(P)
            for a in range(NSB, NSB + 5):
                for k in ((0, 1), (), (2, 3), (4,), (5,))[a - NSB]:
                    out_early(1, k, (2, 3))
                if a == NSB + 1:
                    out_early(1, 5, (0, 1))
                if a == NSB + 3:
                    head_b(HEADS_B - 1)
                tail_b(a)
            rest(1)
            pe.wait_ge(s_ss, 9 * 4 + NT)
            pe.matmul(bank[6][:, :], lhsT=ones[:, :], rhs=ssq[:, :], start=True, stop=False)
            pe.wait_ge(s_sq, 8 * 4 + NT)
            pe.matmul(bank[6][:, :], lhsT=ones[:, :], rhs=sq[:, :], start=False, stop=True).then_inc(s_stat, 1)

        @block.scalar
        def _(act):
            def split_hi(u, slot, gain=False):
                if gain:
                    act.wait_ge(s_wg, u + (1 - U_LAYER))
                else:
                    act.wait_ge(s_wd[slot % 2], 16 * (u // 2) + 16)
                if u > 3:
                    act.wait_ge(s_unit, u - 3)
                act.activation(wh[:, slot, :], wf[:, slot % 2, :], ACT.Copy).then_inc(s_wh, 1)

            def split_hi_pair(P, c, slot):
                act.wait_ge(s_wd[slot % 2], P * 16 + (16 * (c // 2) + 16))
                act.wait_ge(s_unit, P * 2 + (c - 3))
                act.activation(wh[:, slot, :], wf[:, slot % 2, :], ACT.Copy).then_inc(s_wh, 1)

            def square(v, k, src):
                act.wait_ge(s_ss, 9 * v + k + 1)
                act.activation(sq[:, :], src, ACT.Square).then_inc(s_sq, 1)

            def norm(v):
                act.preload_act_table_set("natural_log_exp_and_others")
                act.wait_ge(s_stat, v + 1)
                act.activation(rms[:, :], bank[6][:, :], ACT.Ln, scale=1.0 / D, bias=EPS).then_inc(s_lnr, 1)
                if v in (0, 2):
                    act.activation(rmc[:, :], bank[7][:, 0:4], ACT.Ln, scale=1.0 / D, bias=EPS).then_inc(s_lnr, 1)
                act.wait_ge(s_lnr, NORMED[v])
                act.activation(rms[:, :], rms[:, :], ACT.Exp, scale=-0.5).then_inc(s_rms, 1)
                if v in (0, 2):
                    act.activation(rmc[:, :], rmc[:, :], ACT.Exp, scale=-0.5).then_inc(s_rms, 1)

            def gate_project(L):
                for n in range(NT):
                    u = L * U_LAYER + U_G + n
                    if n > (2, 0)[L]:
                        split_hi(u + 2, (u + 2) % 4, gained(u + 2))
                    if n == 0:
                        norm(2 * L)
                        if L == 0:
                            act.wait_ge(s_lam, 3)
                            act.activation(lam[:, 0:2], lam[:, 0:2], ACT.Exp).then_inc(s_lame, 1)
                        act.preload_act_table(ACT.Silu)
                    act.wait_ge(s_read, L * R_LAYER + R_G + n + 1)
                    if L == 1 and n == 0:
                        act.wait_ge(s_hg, NT)
                    act.activation(tile(gp, n), tmp[:, n % 2, :], ACT.Silu).then_inc(s_silu, 1)

            def values(L):
                act.wait_ge(s_rms, NORMED[2 * L])
                for half in range(2):
                    for j in range(4):
                        u = L * U_LAYER + U_V + 4 * half + j + 2
                        split_hi(u, u % 4, gained(u))
                        if L == 1:
                            hd = 4 * half + j
                            if hd > 0:
                                act.wait_ge(s_brow, hd)
                            act.activation(toh, oh, ACT.Copy, scale=tb[:, hd:hd + 1]).then_inc(s_toh, 1)
                            if hd > 0:
                                bias_out(hd - 1)
                    for i in range(4):
                        if i < 3:
                            act.wait_ge(s_vres, 6 * L + 3 * half + i + 1)
                        else:
                            act.wait_ge(s_unit, L * U_LAYER + U_V + 4 * half + 4)
                        act.activation(ph[1][:, 1024 * i + 512 * half:1024 * i + 512 * half + 512],
                                       bank[V_BANKS[half][i]][:, :], ACT.Copy,
                                       scale=rmc[:, i:i + 1]).then_inc(s_vh, 1)
                if L == 1:
                    bias_out(HEADS_B - 1)

            def bias_out(hd):
                act.wait_ge(s_bst, 2 * hd + 2)
                act.dma_start(scratch[hd], brow[hd % 2]).then_inc(s_bout[hd % 2], 16)

            def stream_hi(v, k, scale):
                act.activation(tile(ph[v % 2], k), tile(h, k), ACT.Copy, scale=scale).then_inc(s_xh, 1)

            def slot_a(a, am, P, Pm, l, dense, attend):
                qh, ql, kh, kl = aqk
                last = isinstance(a, int) and a >= NGA
                if attend and (am - 2) % 3 < 2 and not (isinstance(a, int) and (a < 2 or a > NGA + 1)):
                    g = (am - 2) % 3
                    t = TAILS[g]
                    act.wait_ge(s_ts, tails(P, l - 2))
                    if not (isinstance(a, int) and a < 5):
                        act.wait_ge(s_tri, a - 3)
                    act.activation(tsh[:, g, 0:t.stop - t.start], asp[:, g, t], ACT.Copy).then_inc(s_th, 1)
                if attend and not last:
                    w = GCOLS[am % 3]
                    buf = asp[:, am % 3, 0:w]
                    act.wait_ge(s_z, a + 1)
                    if not (isinstance(a, int) and a < 3):
                        act.wait_ge(s_ll, a - 2)
                        if am % 3 < 2:
                            act.wait_ge(s_tl, tails(P, l - 3))
                        if am % 3 == 0:
                            act.wait_ge(s_ts, tails(P, l - 2))
                    act.activation(buf, bank[2 + am % 4][:, 0:w], ACT.Abs).then_inc(s_abs, 1)
                if attend and not (isinstance(a, int) and (a < 1 or a > NGA)):
                    b = (am - 1) % 12
                    act.wait_ge(s_sp, a)
                    if not (isinstance(a, int) and a < 3):
                        act.wait_ge(s_tri, a - 2)
                    act.activation(alh[:, b % 2, 0:GCOLS[b % 3]], asp[:, b % 3, 0:GCOLS[b % 3]],
                                   ACT.Copy).then_inc(s_lh, 1)
                if attend and not (isinstance(a, int) and (a < 2 or a > NGA + 1)):
                    b = (am - 2) % 12
                    w = GCOLS[b % 3]
                    act.wait_ge(s_tri, a - 1)
                    if not (isinstance(a, int) and a < 4):
                        act.wait_ge(s_pl, a - 3)
                    act.activation(aw[:, b % 2, 0:w], bank[2 + b % 4][:, 0:w], ACT.Exp).then_inc(s_we, 1)
                if dense and l in (0, 2):
                    split_hi_pair(P, U_Q + 2 + l // 2, (2 * Pm + 2 + l // 2) % 4)
                if attend and not last:
                    act.wait_ge(s_abs, a + 1)
                    act.activation(buf, buf, ACT.Exp, scale=-1.0).then_inc(s_ex, 1)
                if dense and l in (2, 4):
                    which = l // 2 - 1
                    act.wait_ge(s_read, P * 2 + (R_Q + which + 1))
                    if not (isinstance(P, int) and P < 2):
                        act.wait_ge(s_z, P * 6 - 6)
                    act.activation((qh, kh)[which][:, Pm, :], tmp[:, which, :], ACT.Copy,
                                   scale=(0.125, 1.0)[which]).then_inc(s_qh, 1)
                if attend and not last:
                    act.wait_ge(s_ex, a + 1)
                    act.activation(buf, buf, ACT.Ln, bias=1.0).then_inc(s_ln, 1)

            def block_a(P, Pm, dense, attend):
                for l in range(6):
                    slot_a(P * 6 + (l - 6), (Pm * 6 + l - 6) % 12, P, Pm, l, dense, attend)

            def split_heads(L, p, done):
                act.wait_ge(s_unit, L * U_LAYER + U_O)
                act.wait_ge(s_og, done)
                act.activation(X(ph[0], p), tile(gp, p), ACT.Copy).then_inc(s_oh, 1)

            def out_project(L):
                v = 2 * L + 1
                for k in range(NT):
                    u = L * U_LAYER + U_O + k + (4 if k < 4 else 3)
                    if k != 4:
                        split_hi(u, u % 4)
                    act.wait_ge(s_read, L * R_LAYER + R_O + k + 1)
                    stream_hi(v, k, gcol(3 + L, k))
                    square(v, k, tile(h, k))
                    if k == 3:
                        embed(L)

            def embed(L):
                act.wait_ge(s_p, 16 * (L + 1))
                act.activation(psplit[L][0][:, :, :], pstage[L], ACT.Copy).then_inc(s_pfh, 1)

            def embed_gate(L):
                for n in range(4):
                    u = L * U_LAYER + U_P + n
                    if n == 0:
                        act.wait_ge(s_read, L * R_LAYER + R_P)
                    for nn in range(2):
                        act.wait_ge(s_ple if nn == 0 else s_unit, 4 * L + n + 1 if nn == 0 else u + 1)
                        act.activation(tile(gp, 2 * n + nn), bank[P_BANKS[(2 * n + nn) % 4]][:, :], ACT.Copy)\
                           .then_inc(s_read, 1)
                    split_hi(u + 3, (u + 3) % 4)
                norm(2 * L + 1)
                act.preload_act_table(ACT.Sigmoid)
                v = 2 * L + 2
                for n in range(NT):
                    u = L * U_LAYER + U_T + n
                    act.wait_ge(s_read, L * R_LAYER + R_T + n + 1)
                    act.activation(tmp[:, n % 2, :], tmp[:, n % 2, :], ACT.Sigmoid).then_inc(s_sig, 1)
                    if u + 3 < UNITS:
                        split_hi(u + 3, (u + 3) % 4, gained(u + 3))
                    act.wait_ge(s_hg, 8 * L + n + 1)
                    if L == 0:
                        stream_hi(v, n, 1.0)
                    square(v, n, tile(h, n))
                    if L == 1 and n < NT - 1:
                        act.activation(tile(gp, n), tile(h, n), ACT.Copy, scale=gcol(5, n)).then_inc(s_hgain, 1)

            def slot_b(a):
                if a % 4 == 0 and 0 <= a < NSB:
                    hd = a // 4 + 1
                    if 2 <= hd < HEADS_B:
                        act.wait_ge(s_ttr, 8 * (hd - 1))
                        load_bias(hd)
                if a >= 8 and a % 4 == 0:
                    hd = (a - 8) // 4
                    act.wait_ge(s_pv, hd + 1)
                    if hd > 0:
                        act.wait_ge(s_nst, hd)
                    act.activation(sq[:, :], bank[7][:, :], ACT.Square).then_inc(s_osq, 1)
                if a >= 9 and a % 4 == 1:
                    hd = (a - 9) // 4
                    act.wait_ge(s_nst, hd + 1)
                    if hd > 0:
                        act.wait_ge(s_og, HEADS_A + 1 + hd)
                    act.activation(ssq[:, :], bank[6][:, :], ACT.Ln, scale=1.0 / 128, bias=EPS)\
                       .then_inc(s_nln, 1)
                    act.wait_ge(s_nln, hd + 1)
                    act.activation(ssq[:, :], ssq[:, :], ACT.Exp, scale=-0.5).then_inc(s_nrm, 1)
                if 0 <= a < NSB:
                    w = S - 128 * (a % 4)
                    act.wait_ge(s_nm, a + 1)
                    c = 8 * (a % 2)
                    act.activation(e1[:, a % 4, 0:w], e1[:, a % 4, 0:w], ACT.Exp, bias=small[:, c + 2:c + 3],
                                   accum_out=small[:, c + 4:c + 5]).then_inc(s_e, 1)
                    act.activation(e2[:, a % 2, 0:w], e2[:, a % 2, 0:w], ACT.Exp, bias=small[:, c + 3:c + 4],
                                   accum_out=small[:, c + 5:c + 6]).then_inc(s_e, 1)

            def copies_b(a):
                for n in range(3):
                    hd, r = divmod(a - 3 - n, 4)
                    if r == 0 and 0 <= hd < HEADS_B:
                        b, c, w = COPIES[n]
                        act.wait_ge(s_tr, 4 * hd + n + 2)
                        if hd > 0:
                            act.wait_ge(s_pv, hd)
                        act.activation(pth[:, c:c + w], bank[b][:, 0:w], ACT.Copy).then_inc(s_pth, 1)

            def load_bias(hd):
                src = scratch[hd].rearrange("p n -> (p n)")[127:127 + 128 * (BW - 1)]
                act.dma_start(bt[:, hd % 2, :], src.rearrange("(p n) -> p n", n=BW - 1)[:, 0:S])\
                   .then_inc(s_bt[hd % 2], 16)

            def weights_b(P, l):
                if P < 4 and l in Q_WEIGHTS:
                    u = U_LAYER + U_Q + 4 * P + Q_WEIGHTS.index(l) + 2
                    split_hi(u, u % 4, gained(u))

            def dense_b(P, l):
                if P < 4:
                    if l in Q_HI:
                        c = Q_HI.index(l)
                        act.wait_ge(s_read, R_LAYER + R_Q + 4 * P + c + 1)
                        if P >= 2:
                            act.wait_ge(s_s, 16 * (P - 1))
                        act.activation(bqk[c][0][:, P % 2, :], tmp[:, c % 2, :], ACT.Copy,
                                       scale=(1.0, 0.125)[c // 2]).then_inc(s_qh, 1)

            act.preload_act_table_set("natural_log_exp_and_others")
            act.dma_start(tmp[:, 0, 0:256], lamp).then_inc(s_lp, 16)
            act.dma_start(sub[:, :], subln).then_inc(s_lp, 16)
            act.wait_ge(s_cst, 16)
            split_hi(0, 0)
            for k in range(NT):
                act.wait_ge(s_x[k // 2], 16)
                stream_hi(0, k, gcol(0, k))
                if k == 1:
                    split_hi(1, 1)
            for u in (2, 3):
                split_hi(u, u)
                for k in range(4 * (u - 2), 4 * (u - 2) + 4):
                    square(0, k, tile(h, k))
            split_hi(4, 0)
            gate_project(0)
            values(0)
            act.preload_act_table_set("natural_log_exp_and_others")
            block_a(0, 0, True, False)
            block_a(1, 1, True, True)
            with act.Fori(1, 4) as it:
                block_a(it * 2, 0, True, True)
                block_a(it * 2 + 1, 1, True, True)
            for l in range(6):
                slot_a(LAST + l, (LAST + l) % 12, 8, 0, l, False, True)
                split_heads(0, l, 2 * l + 3)
                if l in (2, 4):
                    split_hi(U_O + 1 + l // 2, 1 + l // 2)
            for a in range(NGA, NGA + 2):
                slot_a(a, a % 12, 9, 1, a - NGA, False, True)
            split_heads(0, 6, 15)
            split_heads(0, 7, 17)
            act.wait_ge(s_ol, NT)
            act.dma_start(pstage[0], pT[0].rearrange("k p t -> p k t")).then_inc(s_p, 16)
            act.dma_start(oh, onehot).then_inc(s_tb, 16)
            act.wait_ge(s_tb0, 1)
            act.dma_start(tb[0:NB, :], table).then_inc(s_tb, 16)
            out_project(0)
            embed_gate(0)
            gate_project(1)
            act.preload_act_table_set("natural_log_exp_and_others")
            act.wait_ge(s_tb, 32)
            values(1)
            for i in range(2):
                act.wait_ge(s_bout[i], 16 * (HEADS_B // 2))
            load_bias(0)
            load_bias(1)
            for P in range(5):
                for l in range(8):
                    dense_b(P, l)
                    slot_b(8 * P + l - 8)
                    weights_b(P, l)
                    dense_b(P, l + 0.5)
                    if P == 4 and l < 5:
                        split_heads(1, l, HEADS_A + l + 2)
                    if P == 4 and l in (1, 3):
                        split_hi(U_LAYER + U_O + 2 + l // 2, 2 + l // 2)
                    if P == 4 and l == 7:
                        split_heads(1, 5, HEADS_A + 7)
                    copies_b(8 * P + l - 8)
            for a in range(NSB, NSB + 6):
                slot_b(a)
                copies_b(a)
                if a == NSB + 3:
                    split_heads(1, 6, HEADS_A + 8)
            split_heads(1, 7, HEADS_A + 9)
            act.wait_ge(s_ol, 2 * NT)
            act.dma_start(pstage[1], pT[1].rearrange("k p t -> p k t")).then_inc(s_p, 16)
            out_project(1)
            embed_gate(1)
            norm(4)

        @block.vector
        def _(dve):
            def split_lo(u, slot):
                dve.wait_ge(s_wh, u + 1)
                dve.tensor_tensor(wl[:, slot, :], wf[:, slot % 2, :], wh[:, slot, :], ALU.subtract)\
                   .then_inc(s_wl, 1)

            def clear(v):
                if v > 0:
                    dve.wait_ge(s_stat, v)
                dve.memset(ssq[:, :], 0.0).then_inc(s_ss, 1)

            def stream_lo(v, k, gain):
                src, out, hi = tile(h, k), tile(pl[v % 2], k), tile(ph[v % 2], k)
                dve.wait_ge(s_xh, k + (8 * v + 1))
                if gain is None:
                    dve.tensor_tensor(out, src, hi, ALU.subtract).then_inc(s_xl, 1)
                else:
                    dve.scalar_tensor_tensor(out, src, gain, hi, ALU.mult, ALU.subtract).then_inc(s_xl, 1)

            def add_squares(v, k):
                dve.wait_ge(s_sq, k + (8 * v + 1))
                dve.wait_ge(s_ss, k + (9 * v + 1))
                dve.tensor_tensor(ssq[:, :], ssq[:, :], sq[:, :], ALU.add).then_inc(s_ss, 1)

            def scaled(u, b, t):
                dve.wait_ge(s_unit, u + 1)
                dve.tensor_tensor(tmp[:, t, :], bank[b][:, :], rms[:, :], ALU.mult).then_inc(s_read, 1)

            def gate_project(L):
                for n in range(NT):
                    u = L * U_LAYER + U_G + n
                    if n > (2, 0)[L]:
                        split_lo(u + 2, (u + 2) % 4)
                    if n == 0:
                        dve.wait_ge(s_rms, NORMED[2 * L])
                    if n >= 2:
                        dve.wait_ge(s_silu, NT * L + n - 1)
                    scaled(u, G_BANKS[n % 4], n % 2)

            def values(L):
                dve.wait_ge(s_silu, NT * (L + 1))
                for half in range(2):
                    for j in range(4):
                        split_lo(L * U_LAYER + U_V + 4 * half + j + 2, (j + 2) % 4)
                        if L == 1 and 4 * half + j > 0:
                            bias_row(4 * half + j - 1)
                    for i in range(4):
                        dst = slice(UNIT * i + 512 * half, UNIT * i + 512 * half + 512)
                        dve.wait_ge(s_vh, 8 * L + 4 * half + i + 1)
                        dve.scalar_tensor_tensor(pl[1][:, dst], bank[V_BANKS[half][i]][:, :], rmc[:, i:i + 1],
                                                 ph[1][:, dst], ALU.mult, ALU.subtract).then_inc(s_vl, 1)
                if L == 1:
                    bias_row(HEADS_B - 1)

            def bias_row(hd):
                dve.wait_ge(s_brow, hd + 1)
                if hd >= 2:
                    dve.wait_ge(s_bout[hd % 2], 16 * (hd // 2))
                dve.tensor_copy(brow[hd % 2][:, 0:512], bank[4][:, :]).then_inc(s_bst, 1)
                dve.tensor_copy(brow[hd % 2][:, 512:BW], bank[5][:, 0:BW - 512]).then_inc(s_bst, 1)

            def slot_a(a, am, P, Pm, l, dense, attend):
                qh, ql, kh, kl = aqk
                if dense and l in (2, 4):
                    which = l // 2 - 1
                    scaled(P * 2 + (U_Q + which), which, which)
                if dense and l in (3, 5):
                    which = (l - 3) // 2
                    dst, hi = (ql, kl)[which], (qh, kh)[which]
                    dve.wait_ge(s_qh, P * 2 + (which + 1))
                    dve.scalar_tensor_tensor(dst[:, Pm, :], tmp[:, which, :], (0.125, 1.0)[which],
                                             hi[:, Pm, :], ALU.mult, ALU.subtract).then_inc(s_qk, 1)
                if attend and (am - 2) % 3 < 2 and not (isinstance(a, int) and (a < 2 or a > NGA + 1)):
                    g = (am - 2) % 3
                    t = TAILS[g]
                    w = t.stop - t.start
                    dve.wait_ge(s_th, tails(P, l - 2))
                    dve.tensor_tensor(tsl[:, g, 0:w], asp[:, g, t], tsh[:, g, 0:w], ALU.subtract).then_inc(s_tl, 1)
                if attend and not (isinstance(a, int) and (a < 1 or a > NGA)):
                    b = (am - 1) % 12
                    w = GCOLS[b % 3]
                    dve.wait_ge(s_lh, a)
                    dve.tensor_tensor(all_[:, b % 2, 0:w], asp[:, b % 3, 0:w], alh[:, b % 2, 0:w],
                                      ALU.subtract).then_inc(s_ll, 1)
                if attend and not (isinstance(a, int) and (a < 2 or a > NGA + 1)):
                    b = (am - 2) % 12
                    w = GCOLS[b % 3]
                    dve.wait_ge(s_we, a - 1)
                    if not (isinstance(a, int) and a < 4):
                        dve.wait_ge(s_av, a - 3)
                    dve.tensor_copy(awh[:, b % 2, 0:w], aw[:, b % 2, 0:w]).then_inc(s_ph, 1)
                    dve.wait_ge(s_ph, a - 1)
                    dve.tensor_tensor(awl[:, b % 2, 0:w], aw[:, b % 2, 0:w], awh[:, b % 2, 0:w],
                                      ALU.subtract).then_inc(s_pl, 1)
                if attend and not (isinstance(a, int) and (a < 6 or a > NGA + 3)) and (am - 6) % 3 == 0:
                    hd = ((am - 6) // 3) % 2
                    head_out(a, hd, P, l)
                if dense and l in (0, 2):
                    split_lo(P * 2 + (U_Q + 2 + l // 2), (2 * Pm + 2 + l // 2) % 4)
                if attend and not (isinstance(a, int) and a >= NGA):
                    w = GCOLS[am % 3]
                    buf = asp[:, am % 3, 0:w]
                    dve.wait_ge(s_ln, a + 1)
                    dve.scalar_tensor_tensor(buf, bank[2 + am % 4][:, 0:w], 0.0, buf, ALU.max, ALU.add)\
                       .then_inc(s_sp, 1)

            def head_out(a, hd, P, l):
                p = P - 2
                rows = slice(64 * hd, 64 * hd + 64)
                t = gp[rows, p * S:(p + 1) * S] if isinstance(p, int) else gp[rows, bass.ds(p * S, S)]
                dve.wait_ge(s_av, a - 3)
                dve.tensor_tensor(t, bank[6 + hd][rows, :], t, ALU.mult).then_inc(s_og, 1)

            def block_a(P, Pm, dense, attend):
                for l in range(6):
                    slot_a(P * 6 + (l - 6), (Pm * 6 + l - 6) % 12, P, Pm, l, dense, attend)

            def split_heads(L, p):
                dve.wait_ge(s_oh, NT * L + p + 1)
                dve.wait_ge(s_ol, NT * L + p)
                dve.tensor_tensor(X(pl[0], p), tile(gp, p), X(ph[0], p), ALU.subtract).then_inc(s_ol, 1)

            def out_project(L):
                v = 2 * L + 1
                for k in range(NT):
                    u = L * U_LAYER + U_O + k + (4 if k < 4 else 3)
                    if k != 4:
                        split_lo(u, u % 4)
                    dve.wait_ge(s_unit, L * U_LAYER + U_O + k + 1)
                    dve.tensor_tensor(tile(h, k), tile(h, k), bank[O_BANKS[k % 4]][:, :], ALU.add).then_inc(s_read, 1)
                    stream_lo(v, k, gcol(3 + L, k))
                    if k == NT - 1:
                        add_squares(v, k)
                    if k == 4:
                        dve.wait_ge(s_pfh, L + 1)
                        dve.tensor_tensor(psplit[L][1][:, :, :], pstage[L], psplit[L][0][:, :, :],
                                          ALU.subtract).then_inc(s_pfl, 1)

            def embed_gate(L):
                for n in range(4):
                    u = L * U_LAYER + U_P + n
                    split_lo(u + 3, (u + 3) % 4)
                v = 2 * L + 2
                clear(v)
                dve.wait_ge(s_rms, NORMED[2 * L + 1])
                for n in range(NT):
                    u = L * U_LAYER + U_T + n
                    scaled(u, n % 2, n % 2)
                    t = tmp[:, n % 2, :]
                    dve.wait_ge(s_sig, NT * L + n + 1)
                    dve.tensor_tensor(t, t, tile(gp, n), ALU.mult).then_inc(s_gm, 1)
                    dve.wait_ge(s_gm, NT * L + n + 1)
                    dve.tensor_tensor(tile(h, n), tile(h, n), t, ALU.add).then_inc(s_hg, 1)
                    if u + 3 < UNITS:
                        split_lo(u + 3, (u + 3) % 4)
                    if L == 0:
                        stream_lo(v, n, None)
                    if n == NT - 1 and L == 0:
                        add_squares(v, n)

            def combine(a):
                w, c = S - 128 * (a % 4), 8 * (a % 2)
                dve.wait_ge(s_e, 2 * a + 2)
                dve.reciprocal(small[:, c + 6:c + 8], small[:, c + 4:c + 6]).then_inc(s_rc, 1)
                dve.wait_ge(s_rc, a + 1)
                dve.tensor_scalar(small[:, c + 7:c + 8], small[:, c + 7:c + 8], lam[:, 3:4], None, ALU.mult)\
                   .then_inc(s_nr, 1)
                dve.tensor_scalar(e1[:, a % 4, 0:w], e1[:, a % 4, 0:w], small[:, c + 6:c + 7], None, ALU.mult)\
                   .then_inc(s_e1n, 1)
                dve.wait_ge(s_nr, a + 1)
                dve.wait_ge(s_e1n, a + 1)
                dve.scalar_tensor_tensor(e1[:, a % 4, 0:w], e2[:, a % 2, 0:w], small[:, c + 7:c + 8],
                                         e1[:, a % 4, 0:w], ALU.mult, ALU.add).then_inc(s_pr, 1)

            def slot_b(a):
                if 0 <= a < NSB:
                    hd = a // 4
                    w, c = S - 128 * (a % 4), 8 * (a % 2)
                    if a % 4 == 0:
                        dve.wait_ge(s_bt[hd % 2], 16 * (hd // 2) + 16)
                    if a >= 4:
                        dve.wait_ge(s_tr, a - 3)
                    if a >= 2:
                        dve.wait_ge(s_pr, a - 1)
                    for side, buf in enumerate((e1[:, a % 4, 0:w], e2[:, a % 2, 0:w])):
                        dve.wait_ge(s_s, 2 * a + side + 1)
                        dve.tensor_tensor_reduce(buf, bank[2 + side][:, 0:w], bt[:, hd % 2, S - w:S], 1.0, -3e38,
                                                 ALU.add, ALU.max, small[:, c + side:c + side + 1])\
                           .then_inc(s_ttr, 1)
                    dve.wait_ge(s_ttr, 2 * a + 2)
                    dve.tensor_scalar(small[:, c + 2:c + 4], small[:, c:c + 2], -1.0, None, ALU.mult)\
                       .then_inc(s_nm, 1)
                if a >= 10 and a % 4 == 2:
                    hd = (a - 10) // 4
                    dve.wait_ge(s_nrm, hd + 1)
                    dve.tensor_tensor(ssq[:, :], bank[7][:, :], ssq[:, :], ALU.mult).then_inc(s_on, 1)
                results_b(a // 8 + 1, a % 8 + 0.25)
                for n in range(3):
                    hd, r = divmod(a - 4 - n, 4)
                    if r == 0 and 0 <= hd < HEADS_B:
                        b, c, w = COPIES[n]
                        dve.wait_ge(s_pth, 3 * hd + n + 1)
                        dve.tensor_tensor(ptl[:, c:c + w], bank[b][:, 0:w], pth[:, c:c + w], ALU.subtract)\
                           .then_inc(s_pte, 1)
                if 1 <= a < NSB + 1:
                    combine(a - 1)

            def results_b(P, l):
                if P < 4:
                    if l in Q_READ:
                        c = Q_READ.index(l)
                        if 4 * P + c >= 2:
                            dve.wait_ge(s_qk, HEADS_A + 4 * P + c - 1)
                        scaled(U_LAYER + U_Q + 4 * P + c, c % 2, c % 2)
                    if l in Q_LO:
                        c = Q_LO.index(l)
                        dve.wait_ge(s_qh, HEADS_A + 4 * P + c + 1)
                        dve.scalar_tensor_tensor(bqk[c][1][:, P % 2, :], tmp[:, c % 2, :], (1.0, 0.125)[c // 2],
                                                 bqk[c][0][:, P % 2, :], ALU.mult, ALU.subtract)\
                           .then_inc(s_qk, 1)

            def weights_b(P, l):
                if P < 4 and l in Q_WEIGHTS:
                    u = U_LAYER + U_Q + 4 * P + Q_WEIGHTS.index(l) + 2
                    split_lo(u, u % 4)

            dve.memset(tb[NB:NB + 1, :], NEG).then_inc(s_tb0, 1)
            dve.wait_ge(s_trf, 2)
            dve.tensor_scalar(neg1[:, :], ones[:, :], -1.0, None, ALU.mult).then_inc(s_one, 1)
            dve.tensor_copy(tri[:, :], trif[:, :]).then_inc(s_one, 1)
            for i in range(2):
                dve.tensor_scalar(future[:, i, :], trif[:, :], -NEG, None, ALU.mult).then_inc(s_one, 1)
            dve.memset(small[:, :], 0.0).then_inc(s_og, 1)
            clear(0)
            dve.wait_ge(s_lp, 32)
            dve.tensor_tensor(lpp, lp[:, 0:4:2, :], lp[:, 1:4:2, :], ALU.mult).then_inc(s_lam, 1)
            dve.wait_ge(s_lam, 1)
            dve.tensor_reduce(lam[:, 0:2], lpp, AX.X, ALU.add).then_inc(s_lam, 1)
            dve.tensor_scalar(sub[:, :], sub[:, :], 1.0 - LAM_INIT, None, ALU.mult).then_inc(s_lam, 1)
            dve.wait_ge(s_idn, 2)
            dve.tensor_copy(idr[:, :], trif[:, :]).then_inc(s_one, 1)
            dve.wait_ge(s_cst, 16)
            split_lo(0, 0)
            for k in range(NT):
                stream_lo(0, k, gcol(0, k))
                if k == 1:
                    split_lo(1, 1)
            for u in (2, 3):
                split_lo(u, u)
                for k in range(4 * (u - 2), 4 * (u - 2) + 4):
                    add_squares(0, k)
            split_lo(4, 0)
            gate_project(0)
            values(0)
            block_a(0, 0, True, False)
            block_a(1, 1, True, True)
            with dve.Fori(1, 4) as it:
                block_a(it * 2, 0, True, True)
                block_a(it * 2 + 1, 1, True, True)
            for l in range(6):
                slot_a(LAST + l, (LAST + l) % 12, 8, 0, l, False, True)
                if l in (2, 4):
                    split_lo(U_O + 1 + l // 2, 1 + l // 2)
            for a in range(NGA, NGA + 4):
                slot_a(a, a % 12, 9, 1, a - NGA, False, True)
            split_heads(0, 6)
            split_heads(0, 7)
            clear(1)
            out_project(0)
            embed_gate(0)
            gate_project(1)
            dve.wait_ge(s_lame, 1)
            dve.tensor_tensor(lam[:, 2:3], lam[:, 1:2], lam[:, 0:1], ALU.subtract).then_inc(s_lam, 1)
            dve.wait_ge(s_lam, 4)
            dve.tensor_scalar(lam[:, 3:4], lam[:, 2:3], -LAM_INIT, None, ALU.add).then_inc(s_lam, 1)
            values(1)
            dve.wait_ge(s_lam, 5)
            for P in range(5):
                for l in range(8):
                    results_b(P, l)
                    slot_b(8 * P + l - 8)
                    weights_b(P, l)
                    results_b(P, l + 0.5)
                    if P == 4 and l in (1, 3):
                        split_lo(U_LAYER + U_O + 2 + l // 2, 2 + l // 2)
            for a in range(NSB, NSB + 7):
                slot_b(a)
                if a == NSB + 3:
                    split_heads(1, 6)
            split_heads(1, 7)
            clear(3)
            out_project(1)
            embed_gate(1)
            dve.wait_ge(s_rms, NORMED[4])
            dve.wait_ge(s_hgain, NT - 1)
            for k in FINAL[0][:-1]:
                dve.tensor_tensor(tile(h, k), tile(gp, k), rms[:, :], ALU.mult).then_inc(s_fin[0], 1)
            dve.scalar_tensor_tensor(tile(h, NT - 1), tile(h, NT - 1), gcol(5, NT - 1), rms[:, :],
                                     ALU.mult, ALU.mult).then_inc(s_fin[0], 1)

        @block.gpsimd
        def _(pool):
            pool.memset(ones[:, :], 1.0).then_inc(s_trf, 1)
            pool.memset(trif[:, :], -1.0).then_inc(s_t0, 1)
            pool.wait_ge(s_t0, 1)
            pool.affine_select(out=trif[:, :], in_=trif[:, :], compare_op=ALU.is_ge, fill=0.0, base=0,
                               pattern=[[-1, 128]], channel_multiplier=1).then_inc(s_trf, 1)
            pool.wait_ge(s_one, 4)
            pool.memset(trif[:, :], 0.0).then_inc(s_idn, 1)
            pool.wait_ge(s_idn, 1)
            pool.affine_select(out=trif[:, :], in_=trif[:, :], compare_op=ALU.not_equal, fill=1.0, base=0,
                               pattern=[[-1, 128]], channel_multiplier=1).then_inc(s_idn, 1)

            def add_squares(v, k):
                pool.wait_ge(s_sq, 8 * v + k + 1)
                pool.wait_ge(s_ss, 9 * v + k + 1)
                pool.tensor_tensor(ssq[:, :], ssq[:, :], sq[:, :], ALU.add).then_inc(s_ss, 1)

            def value_columns(n, slot):
                for src, dst in ((ph[1], vph), (pl[1], vpl)):
                    view = src[:, :].rearrange("p (i c) -> p i c", i=4)
                    pool.tensor_copy(dst[:, slot, :, :], view[:, :, bass.ds(n * 128, 128)]).then_inc(s_vp, 1)

            def pair_columns(P, Pm):
                if not (isinstance(P, int) and P < 2):
                    pool.wait_ge(s_av, P * 6 - 6)
                value_columns(P, Pm)

            def tail_sum(P, m):
                g = m % 3
                pool.wait_ge(s_ll, P * 6 + (m - 5))
                if g == 1:
                    pool.wait_ge(s_ts, tails(P, m - 1))
                own, later = ((256, 384), (0, 128)) if g == 0 else ((128, 384), (128, 384))
                out = asp[:, g, own[0]:own[1]]
                pool.tensor_tensor(out, out, asp[:, 0, later[0]:later[1]], ALU.add).then_inc(s_ts, 1)

            def block_a(P, Pm):
                for m in (0, 1):
                    tail_sum(P, m)
                pair_columns(P, Pm)
                for m in (3, 4):
                    tail_sum(P, m)

            def split_heads(L, p):
                pool.wait_ge(s_oh, NT * L + p + 1)
                pool.tensor_tensor(X(pl[0], p), tile(gp, p), X(ph[0], p), ALU.subtract).then_inc(s_ol, 1)

            pool.wait_ge(s_vl, 8)
            pair_columns(0, 0)
            block_a(1, 1)
            with pool.Fori(1, 4) as it:
                block_a(it * 2, 0)
                block_a(it * 2 + 1, 1)
            for l in range(6):
                split_heads(0, l)
                if l % 3 < 2:
                    tail_sum(8, l)

            def gain(u, g, per):
                k0 = 0 if per == 128 else 2 * (u % 4)
                t = wf[:, u % 2, :].rearrange("p (k c) -> p k c", c=per)
                n = UNIT // per
                pool.wait_ge(s_wd[u % 2], 16 * (u // 2) + 16)
                col = gn[:, g * NT + k0:g * NT + k0 + n]\
                      .rearrange("p (k o) -> p k o", o=1).to_broadcast([128, n, per])
                pool.tensor_tensor(t, t, col, ALU.mult).then_inc(s_wg, 1)

            def gate_head(a):
                hd = (a - 10) // 4
                pool.wait_ge(s_on, hd + 1)
                pool.tensor_tensor(tile(gp, hd), ssq[:, :], tile(gp, hd), ALU.mult).then_inc(s_og, 1)

            for v in (1, 2):
                for k in range(NT - 1):
                    if v == 2 and k >= 5:
                        gain(U_LAYER + U_G + k - 5, 2, 128)
                    add_squares(v, k)
            for n in range(2, U_V):
                gain(U_LAYER + U_G + n, 2, 128)
            for n in range(U_Q - U_V):
                gain(U_LAYER + U_V + n, 1, 512)
                if n < 4:
                    for m in range(2 * n, 2 * n + 2):
                        pool.wait_ge(s_silu, NT + m + 1)
                        if m == 0:
                            pool.wait_ge(s_lam, 3)
                        pool.tensor_scalar(tile(gp, m), tile(gp, m), sub[:, 0:1], None, ALU.mult).then_inc(s_silc, 1)
            q_units = [(U_LAYER + U_Q + n, 1 if n % 4 < 2 else 2) for n in range(16)]
            for n in range(2):
                gain(*q_units.pop(0), 128)
            pool.wait_ge(s_vl, 16)
            for P in range(5):
                for l in range(8):
                    a = 8 * P + l - 8
                    if P < 4 and l in Q_WEIGHTS and q_units:
                        gain(*q_units.pop(0), 128)
                    if a >= 10 and a % 4 == 2:
                        gate_head(a)
                    if P == 4 and l < 5:
                        split_heads(1, l)
                    if P == 4 and l == 7:
                        split_heads(1, 5)
            for a in range(NSB, NSB + 7):
                if a % 4 == 2:
                    gate_head(a)
            for v in (3, 4):
                for k in range(NT - 1):
                    add_squares(v, k)
            pool.wait_ge(s_rms, NORMED[4])
            pool.wait_ge(s_hgain, NT - 1)
            for k in FINAL[1]:
                pool.tensor_tensor(tile(h, k), tile(gp, k), rms[:, :], ALU.mult).then_inc(s_fin[1], 1)


def bucket_rows():
    dist = 511 - np.arange(BW)
    n = np.maximum(dist, 0)
    nf = np.maximum(n, 1).astype(np.float32)
    half = NB // 2
    large = half + (np.log(nf / half) / np.float32(math.log(128 / half)) * (NB - half)).astype(np.int32)
    b = np.where(n < half, n, np.minimum(large, NB - 1))
    rows = np.zeros((NB + 1, BW), np.float32)
    for j in range(BW):
        rows[b[j] if dist[j] >= 0 else NB, j] = 1.0
    return rows


def kernel(x, p, attn_norm, w_in_a, w_out_a, kv_norm, w_kv, w_q_b, diff_lambda, diff_subln, w_out_b,
           rel_bias, ple_norm, w_ple_proj, w_ple_gate, final_norm):
    import concourse.bacc as _bacc
    from concourse.bass_utils import run_bass_kernel_spmd as _run

    def cols(w):
        k, n = w.shape
        return w.reshape(k // 128, 128, n // 128, 128).transpose(2, 1, 0, 3).reshape(n // 128, 128, -1)

    def slabs(w):
        return w.reshape(4, 2, 128, w.shape[1] // 512, 512).transpose(3, 0, 2, 1, 4).reshape(-1, 128, UNIT)

    def pairs(w):
        u = cols(w).reshape(4, 2, 128, 256).transpose(0, 2, 1, 3).reshape(4, 128, 512)
        return np.concatenate([u, np.zeros_like(u)], axis=2)

    def woven(*parts):
        return np.stack(parts, axis=1).reshape(-1, 128, UNIT)

    w_in, w_oa, w_qb, w_ob = w_in_a[0], w_out_a[0], w_q_b[0], w_out_b[0]
    units = np.concatenate([
        cols(w_in[:, 3 * D:]), slabs(w_in[:, 2 * D:3 * D]),
        woven(cols(w_in[:, :D]), cols(w_in[:, D:2 * D])),
        cols(w_oa), pairs(w_ple_proj[0]), cols(w_ple_gate[0]),
        cols(w_qb[:, D:]), slabs(w_kv[:, D:]),
        woven(cols(w_kv[:, :512]), cols(w_kv[:, 512:D]), cols(w_qb[:, :512]), cols(w_qb[:, 512:D])),
        cols(w_ob), pairs(w_ple_proj[1]), cols(w_ple_gate[1])])
    gains = np.stack([attn_norm[0], kv_norm, attn_norm[1], ple_norm[0], ple_norm[1], final_norm])
    arrays = {
        "xT": x[0].T.reshape(NT, 128, S),
        "pT": p[:, 0].transpose(0, 2, 1).reshape(2, DP // 128, 128, S),
        "w_units": units,
        "gains": gains.reshape(6, NT, 128).transpose(2, 0, 1).reshape(128, 6 * NT),
        "subln": diff_subln.reshape(128, 1),
        "lamp": np.broadcast_to(diff_lambda.reshape(1, 256), (128, 256)),
        "table": rel_bias,
        "onehot": bucket_rows(),
    }
    arrays = {f"in_{n}": np.ascontiguousarray(v) for n, v in arrays.items()}
    nc = _bacc.Bacc("TRN2", target_bir_lowering=False, num_devices=1)
    ins = [nc.dram_tensor(n, v.shape, F32, kind="ExternalInput").ap() for n, v in arrays.items()]
    scratch = nc.dram_tensor("bias_rows", (HEADS_B, 128, BW), F32, kind="Internal").ap()
    outT = nc.dram_tensor("outT", (NT, 128, S), F32, kind="ExternalOutput").ap()
    build(nc, *ins, scratch, outT)
    got = _run(nc, [arrays], core_ids=[0]).results[0]["outT"]
    return np.ascontiguousarray(got.reshape(D, S).T).reshape(1, S, D)
```
